# Optimizing a Trainium2 kernel written in Bass

```python
import math
import jax, jax.numpy as jnp
from jax import lax
import numpy as np

D_MODEL = 2048
BATCH = 1
SEQ = 256
DEPTH = 1

CHUNK = 64
EPS = 1e-6
N_MOD = 9
D_FF = 5632
SSD_D_INNER = 2048
SSD_HEAD_DIM = 64
SSD_HEADS = SSD_D_INNER // SSD_HEAD_DIM
SSD_GROUPS = 8
SSD_STATE = 128
SSD_CONV = 4
SSD_XBC = SSD_D_INNER + 2 * SSD_GROUPS * SSD_STATE
ATT_HEADS = 16
ATT_KV_HEADS = 4
ATT_HEAD_DIM = 128
ATT_WIDTH = ATT_HEADS * ATT_HEAD_DIM
ATT_KV_WIDTH = ATT_KV_HEADS * ATT_HEAD_DIM
IDX_HEADS = 16
IDX_HEAD_DIM = 64
TOPK_MAX = 256
Q_BLOCK = 128
ALIBI_MAX_BIAS = 8.0
N_BRANCH = 2
IN_SPLITS = (SSD_D_INNER, SSD_XBC, SSD_HEADS, ATT_WIDTH, ATT_KV_WIDTH, ATT_KV_WIDTH,
             IDX_HEADS * IDX_HEAD_DIM, IDX_HEAD_DIM, IDX_HEADS, N_BRANCH * D_MODEL)
D_IN_PROJ = sum(IN_SPLITS)

kernel_name = 'hybrid_ssd_dsa_macaron_block'

def _rms(x, w):
    xf = x.astype(jnp.float32)
    y = xf * lax.rsqrt(jnp.mean(xf * xf, axis=-1, keepdims=True) + EPS)
    return (y * w.astype(jnp.float32)).astype(x.dtype)

def _modulate(x, shift, scale):
    return x * (1 + scale[:, None, :]) + shift[:, None, :]

def _swiglu(x, w1, w3, w2):
    return (jax.nn.silu(x @ w1) * (x @ w3)) @ w2

def _split_cols(u):
    outs, off = [], 0
    for n in IN_SPLITS:
        outs.append(u[..., off:off + n])
        off += n
    return outs

def _causal_dwconv(x, w, b):
    k, ch = w.shape
    y = lax.conv_general_dilated(x, w[:, None, :].astype(x.dtype), window_strides=(1,),
                                 padding=[(k - 1, 0)], dimension_numbers=('NWC', 'WIO', 'NWC'),
                                 feature_group_count=ch)
    return y + b

def _ssd_scan(xdt, dta, bm, cm):
    b, L, G, R, P = xdt.shape
    N = bm.shape[-1]
    nc = L // CHUNK

    def to_chunks(a):
        return jnp.moveaxis(a.reshape(b, nc, CHUNK, *a.shape[2:]), 1, 0)

    causal = jnp.tril(jnp.ones((CHUNK, CHUNK), bool))[None, :, :, None, None]

    def step(state, inp):
        xc, ac, bc, cc = inp
        acum = jnp.cumsum(ac, axis=1)
        seg = acum[:, :, None] - acum[:, None, :]
        decay = jnp.exp(jnp.where(causal, seg, -jnp.inf))
        cb = jnp.einsum('btgn,bsgn->btsg', cc, bc)
        y_diag = jnp.einsum('btsg,btsgr,bsgrp->btgrp', cb, decay, xc)
        y_off = jnp.einsum('btgn,bgrpn,btgr->btgrp', cc, state, jnp.exp(acum))
        a_last = acum[:, -1]
        w_s = jnp.exp(a_last[:, None] - acum)
        new_state = state * jnp.exp(a_last)[..., None, None] + jnp.einsum(
            'bsgn,bsgr,bsgrp->bgrpn', bc, w_s, xc)
        return new_state.astype(jnp.float32), (y_diag + y_off).astype(jnp.float32)

    state0 = jnp.zeros((b, G, R, P, N), jnp.float32)
    xs = (to_chunks(xdt), to_chunks(dta), to_chunks(bm), to_chunks(cm))
    _, ys = lax.scan(step, state0, xs)
    return jnp.moveaxis(ys, 0, 1).reshape(b, L, G, R, P).astype(xdt.dtype)

def _ssd_branch(z, xbc, dt_raw, conv_w, conv_b, dt_bias, a_log, d_skip, norm_w):
    b, L, _ = z.shape
    R = SSD_HEADS // SSD_GROUPS
    xbc = jax.nn.silu(_causal_dwconv(xbc, conv_w, conv_b))
    xs = xbc[..., :SSD_D_INNER].reshape(b, L, SSD_GROUPS, R, SSD_HEAD_DIM)
    bm = xbc[..., SSD_D_INNER:SSD_D_INNER + SSD_GROUPS * SSD_STATE].reshape(b, L, SSD_GROUPS, SSD_STATE)
    cm = xbc[..., SSD_D_INNER + SSD_GROUPS * SSD_STATE:].reshape(b, L, SSD_GROUPS, SSD_STATE)
    dt = jax.nn.softplus((dt_raw + dt_bias).astype(jnp.float32)).reshape(b, L, SSD_GROUPS, R)
    a = -jnp.exp(a_log.astype(jnp.float32)).reshape(SSD_GROUPS, R)
    y = _ssd_scan(xs * dt[..., None].astype(xs.dtype), dt * a, bm, cm)
    y = y + d_skip.reshape(SSD_GROUPS, R)[:, :, None] * xs
    y = y.reshape(b, L, SSD_D_INNER) * jax.nn.silu(z)
    y = _rms(y.reshape(b, L, SSD_GROUPS, SSD_D_INNER // SSD_GROUPS),
             norm_w.reshape(SSD_GROUPS, SSD_D_INNER // SSD_GROUPS))
    return y.reshape(b, L, SSD_D_INNER)

def _alibi_slopes():
    h = jnp.arange(1, ATT_HEADS + 1, dtype=jnp.float32)
    return jnp.exp2(-ALIBI_MAX_BIAS * h / ATT_HEADS)

def _dsa_branch(q, k, v, q_idx, k_idx, w_idx, positions, q_norm_w, k_norm_w):
    b, L, _ = q.shape
    rq = ATT_HEADS // ATT_KV_HEADS
    top_k = min(TOPK_MAX, L // 4)
    q = _rms(q.reshape(b, L, ATT_HEADS, ATT_HEAD_DIM), q_norm_w).reshape(b, L, ATT_KV_HEADS, rq, ATT_HEAD_DIM)
    k = _rms(k.reshape(b, L, ATT_KV_HEADS, ATT_HEAD_DIM), k_norm_w)
    v = v.reshape(b, L, ATT_KV_HEADS, ATT_HEAD_DIM)
    q_idx = q_idx.reshape(b, L, IDX_HEADS, IDX_HEAD_DIM)
    key_chunk = positions // CHUNK
    slopes = _alibi_slopes().reshape(ATT_KV_HEADS, rq)
    idx_scale = (IDX_HEAD_DIM * IDX_HEADS) ** -0.5
    att_scale = ATT_HEAD_DIM ** -0.5
    nblk = L // Q_BLOCK
    gather = jax.vmap(lambda arr, ix: arr[ix])

    def blocks(a):
        return jnp.moveaxis(a.reshape(b, nblk, Q_BLOCK, *a.shape[2:]), 1, 0)

    def one_block(inp):
        qb, qib, wb, pb = inp
        qchunk = pb // CHUNK
        rel = jax.nn.relu(jnp.einsum('bthd,bsd->bths', qib, k_idx))
        score = jnp.einsum('bths,bth->bts', rel, wb).astype(jnp.float32) * idx_scale
        admissible = key_chunk[:, None, :] <= qchunk[:, :, None]
        score = jnp.where(admissible, score, -jnp.inf)
        _, sel = lax.top_k(score, top_k)
        k_sel = gather(k, sel)
        v_sel = gather(v, sel)
        p_sel = gather(positions, sel)
        valid = (p_sel // CHUNK) <= qchunk[..., None]
        dist = jnp.abs(pb[..., None] - p_sel).astype(jnp.float32)
        logits = jnp.einsum('btgrd,btkgd->btgrk', qb, k_sel).astype(jnp.float32) * att_scale
        logits = logits - slopes[None, None, :, :, None] * dist[:, :, None, None, :]
        logits = jnp.where(valid[:, :, None, None, :], logits, -jnp.inf)
        probs = jax.nn.softmax(logits, axis=-1).astype(v.dtype)
        return jnp.einsum('btgrk,btkgd->btgrd', probs, v_sel)

    out = lax.map(one_block, (blocks(q), blocks(q_idx), blocks(w_idx), blocks(positions)))
    return jnp.moveaxis(out, 0, 1).reshape(b, L, ATT_WIDTH)

def _mixer(hn, positions, w_in, conv_w, conv_b, dt_bias, a_log, d_skip, ssd_norm,
           q_norm_w, k_norm_w, w_br_ssd, w_br_att, w_out):
    b, L, _ = hn.shape
    u = hn @ w_in
    z, xbc, dt_raw, q, k, v, q_idx, k_idx, w_idx, gate_logits = _split_cols(u)
    y_ssd = _ssd_branch(z, xbc, dt_raw, conv_w, conv_b, dt_bias, a_log, d_skip, ssd_norm)
    y_att = _dsa_branch(q, k, v, q_idx, k_idx, w_idx, positions, q_norm_w, k_norm_w)
    g = jax.nn.sigmoid(gate_logits).reshape(b, L, N_BRANCH, D_MODEL)
    merged = g[:, :, 0] * (y_ssd @ w_br_ssd) + g[:, :, 1] * (y_att @ w_br_att)
    return merged @ w_out

def setup_inputs(seed: int = 0) -> dict:
    key = jax.random.key(seed)
    ks = jax.random.split(key, 32)
    f32 = jnp.float32

    def nrm(k, shape, fan_in, gain=1.0):
        return jax.random.normal(k, shape, f32) * (gain * fan_in ** -0.5)

    def gain(k, shape):
        return 1.0 + 0.02 * jax.random.normal(k, shape, f32)

    x = jax.random.normal(ks[0], (BATCH, SEQ, D_MODEL), f32)
    c = jax.random.normal(ks[1], (BATCH, D_MODEL), f32)
    start = jax.random.randint(ks[2], (BATCH, 1), 0, 8, jnp.int32) * CHUNK
    positions = (start + jnp.arange(SEQ, dtype=jnp.int32)[None, :]).astype(jnp.int32)
    dt0 = jnp.exp(jax.random.uniform(ks[3], (DEPTH, SSD_HEADS), f32, math.log(1e-3), math.log(1e-1)))
    return {
        'x': x,
        'c': c,
        'positions': positions,
        'w_ada': nrm(ks[4], (DEPTH, D_MODEL, N_MOD * D_MODEL), D_MODEL, 0.5),
        'b_ada': 0.01 * jax.random.normal(ks[5], (DEPTH, N_MOD * D_MODEL), f32),
        'norm_ffn1': gain(ks[6], (DEPTH, D_MODEL)),
        'ffn1_w1': nrm(ks[7], (DEPTH, D_MODEL, D_FF), D_MODEL),
        'ffn1_w3': nrm(ks[8], (DEPTH, D_MODEL, D_FF), D_MODEL),
        'ffn1_w2': nrm(ks[9], (DEPTH, D_FF, D_MODEL), D_FF),
        'norm_mix': gain(ks[10], (DEPTH, D_MODEL)),
        'w_in': nrm(ks[11], (DEPTH, D_MODEL, D_IN_PROJ), D_MODEL),
        'ssd_conv_w': nrm(ks[12], (DEPTH, SSD_CONV, SSD_XBC), SSD_CONV),
        'ssd_conv_b': 0.01 * jax.random.normal(ks[13], (DEPTH, SSD_XBC), f32),
        'ssd_dt_bias': dt0 + jnp.log(-jnp.expm1(-dt0)),
        'ssd_a_log': jnp.log(jax.random.uniform(ks[14], (DEPTH, SSD_HEADS), f32, 1.0, 16.0)),
        'ssd_d': gain(ks[15], (DEPTH, SSD_HEADS)),
        'ssd_norm': gain(ks[16], (DEPTH, SSD_D_INNER)),
        'q_norm': gain(ks[17], (DEPTH, ATT_HEAD_DIM)),
        'k_norm': gain(ks[18], (DEPTH, ATT_HEAD_DIM)),
        'w_br_ssd': nrm(ks[19], (DEPTH, SSD_D_INNER, D_MODEL), SSD_D_INNER),
        'w_br_att': nrm(ks[20], (DEPTH, ATT_WIDTH, D_MODEL), ATT_WIDTH),
        'w_out': nrm(ks[21], (DEPTH, D_MODEL, D_MODEL), D_MODEL),
        'norm_ffn2': gain(ks[22], (DEPTH, D_MODEL)),
        'ffn2_w1': nrm(ks[23], (DEPTH, D_MODEL, D_FF), D_MODEL),
        'ffn2_w3': nrm(ks[24], (DEPTH, D_MODEL, D_FF), D_MODEL),
        'ffn2_w2': nrm(ks[25], (DEPTH, D_FF, D_MODEL), D_FF),
    }

def reference(x, c, positions, w_ada, b_ada, norm_ffn1, ffn1_w1, ffn1_w3, ffn1_w2, norm_mix, w_in,
              ssd_conv_w, ssd_conv_b, ssd_dt_bias, ssd_a_log, ssd_d, ssd_norm, q_norm, k_norm,
              w_br_ssd, w_br_att, w_out, norm_ffn2, ffn2_w1, ffn2_w3, ffn2_w2):
    h = x
    c_act = jax.nn.silu(c)
    for l in range(DEPTH):
        mod = c_act @ w_ada[l] + b_ada[l]
        sh1, sc1, g1, sh2, sc2, g2, sh3, sc3, g3 = jnp.split(mod, N_MOD, axis=-1)
        hn = _modulate(_rms(h, norm_ffn1[l]), sh1, sc1)
        h = h + 0.5 * g1[:, None, :] * _swiglu(hn, ffn1_w1[l], ffn1_w3[l], ffn1_w2[l])
        hn = _modulate(_rms(h, norm_mix[l]), sh2, sc2)
        h = h + g2[:, None, :] * _mixer(hn, positions, w_in[l], ssd_conv_w[l], ssd_conv_b[l],
                                        ssd_dt_bias[l], ssd_a_log[l], ssd_d[l], ssd_norm[l],
                                        q_norm[l], k_norm[l], w_br_ssd[l], w_br_att[l], w_out[l])
        hn = _modulate(_rms(h, norm_ffn2[l]), sh3, sc3)
        h = h + 0.5 * g3[:, None, :] * _swiglu(hn, ffn2_w1[l], ffn2_w3[l], ffn2_w2[l])
    return h


_drawn_inputs = setup_inputs


def setup_inputs(seed=0):
    import zlib

    import numpy as np

    out = dict(_drawn_inputs(seed))
    spreads = {}
    factors = {'b_ada': 4.66,
     'norm_ffn1': 8.0,
     'norm_mix': 4.638,
     'ssd_conv_b': 64.0,
     'ssd_d': 64.0,
     'ssd_norm': 64.0,
     'q_norm': 23.807,
     'k_norm': 24.474,
     'norm_ffn2': 22.068}
    for name, (base, spread) in spreads.items():
        noise = np.random.default_rng([zlib.crc32(name.encode()), seed]).standard_normal(out[name].shape)
        drawn = base * np.exp(spread * noise) if base else spread * noise
        out[name] = __import__('jax').numpy.asarray(drawn.astype(out[name].dtype))
    for name, factor in factors.items():
        out[name] = (out[name] * factor).astype(out[name].dtype)
    return out
```

```python
from contextlib import ExitStack

import numpy as np

import concourse.bass as bass
from concourse import mybir

F32 = mybir.dt.float32
F32R = mybir.dt.float32r
I32 = mybir.dt.int32
ALU = mybir.AluOpType
ACT = mybir.ActivationFunctionType
AX = mybir.AxisListType

P = 128
T = 256
HALF = T // P
D = 2048
KT = D // P
FF = 5632
NB = 512
FBLK = FF // NB
QB = D // NB
UNIT = 2 * NB
UPB = KT // 2
RAW = 4
SPLIT = 4
LAG = 3
EPS = 1e-6
CHUNK = 64

N_MOD = 9
ADA_COLS = 1024
ADA_RING = 4
N_ADA = N_MOD * D // ADA_COLS
ADA_FIRST = 4
ADA_PEELED = 2
TRIPS = (FBLK - 3) // 2
ADA_MIX = ADA_FIRST + ADA_PEELED + TRIPS
ADA_MIXED = 3
ADA_MERGE = ADA_MIX + ADA_MIXED
ADA_FFN2 = ADA_MERGE + QB - 1

SSD_H = 32
GROUPS = 8
Z0 = 0
XS0 = 2048
B0 = 4096
C0 = 5120
DT0 = 6144
Q0 = 6176
K0 = 8224
V0 = 8736
QI0 = 9248
KI0 = 10272
WI0 = 10336
G0 = 10352
HEADS = 16
KVH = 4
HD = 128
IDX_H = 16
TOPK = min(256, T // 4)
NEG = -1.0e30
TAKEN = -3.0e38
MASKED = 1.0e30


class At:

    def __init__(self, n0, per=0, trip=0):
        self.n0, self.per, self.trip = n0, per, trip

    def __add__(self, k):
        return At(self.n0 + k, self.per, self.trip)

    def slot(self, ring):
        assert self.per % ring == 0
        return self.n0 % ring

    def count(self, each=1, plus=0):
        n = self.n0 // each + plus
        if self.per == 0:
            return n
        assert self.per % each == 0
        return self.trip * (self.per // each) + n


def build(nc, x, c, positions, w_ada, b_ada, norm_ffn1, ffn1_w1, ffn1_w3, ffn1_w2, norm_mix, w_in,
          ssd_conv_w, ssd_conv_b, ssd_dt_bias, ssd_a_log, ssd_d, ssd_norm, q_norm, k_norm,
          w_br_ssd, w_br_att, w_out, norm_ffn2, ffn2_w1, ffn2_w3, ffn2_w2, out):
    ctx = ExitStack()
    base = [0]

    origin = (nc.sbuf_base + 63) // 64 * 64

    def place(name, offset, shape, dt=F32):
        return nc.alloc_sbuf_tensor_at(name, [P, *shape], dt, offset=origin + offset)

    def region(size):
        at = base[0]
        base[0] += (size + 31) // 32 * 32
        return at

    KB = 1024
    raw = place("raw", region(RAW * UNIT * 4), [RAW, UNIT])
    w_hi = place("w_hi", region(SPLIT * UNIT * 4), [SPLIT, UNIT], F32R)
    w_lo = place("w_lo", region(SPLIT * UNIT * 4), [SPLIT, UNIT], F32R)
    xT_hi = place("xT_hi", region(KT * T * 4), [KT, T], F32R)
    xT_lo = place("xT_lo", region(KT * T * 4), [KT, T], F32R)
    xT_raw = place("xT_raw", base[0] - KT * T * 4, [KT, T])
    at_h = region(16 * KB)
    h = place("h", at_h, [HALF, D])
    at_y = region(16 * KB)
    y = place("y", at_y, [HALF, D])
    vecT = place("vecT", region(114 * 4), [114])
    convT = place("convT", region(128 * 4), [128])
    badaT = place("badaT", region(144 * 4), [144])
    modT = place("modT", region(144 * 4), [144])
    cact = place("cact", region(KT * 4), [KT])
    ident = place("ident", region(P * 4), [P])
    upper = place("upper", region(P * 4), [P])
    ones = place("ones", region(P * 4), [P])
    scale_col = place("scale_col", region(KT * 4), [KT])
    ssum = place("ssum", region(8 * 4), [HALF, QB])
    row_sums = place("row_sums", region(8), [HALF])
    rstd = place("rstd", region(8), [HALF])
    rbase = place("rbase", region(8), [HALF])
    mhalf = place("mhalf", region(8 * 4), [8])
    key_pos = place("key_pos", region(T * 4), [T])
    key_chunk = place("key_chunk", region(T * 4), [T])
    query_pos = place("query_pos", region(8), [HALF])
    query_chunk = place("query_chunk", region(8), [HALF])
    dt_bias = place("dt_bias", region(SSD_H * 4), [SSD_H])
    a_exp = place("a_exp", region(SSD_H * 4), [SSD_H])
    skip = place("skip", region(SSD_H * 4), [SSD_H])
    kiT = place("kiT", region(T * 4), [T])
    wi = place("wi", region(HALF * IDX_H * 4), [HALF, IDX_H])
    dt = place("dt", region(HALF * SSD_H * 4), [HALF, SSD_H])
    dta = place("dta", region(HALF * SSD_H * 4), [HALF, SSD_H])
    sp_v = place("sp_v", region(HALF * SSD_H * 4), [HALF, SSD_H])
    sp_e = place("sp_e", region(HALF * SSD_H * 4), [HALF, SSD_H])
    sp_s = place("sp_s", region(HALF * SSD_H * 4), [HALF, SSD_H])
    sp_p = place("sp_p", region(HALF * SSD_H * 4), [HALF, SSD_H])
    acum = place("acum", region(3 * SSD_H * 4), [3, SSD_H])
    q_scale = place("q_scale", region(4), [1])
    y_sum = place("y_sum", region(8), [HALF])
    y_base = place("y_base", region(8), [HALF])
    y_rstd = place("y_rstd", region(8), [HALF])
    h_sum = place("h_sum", region(32), [8])
    h_base = place("h_base", region(32), [8])
    h_rstd = place("h_rstd", region(32), [8])
    top8 = place("top8", region(HALF * 32), [HALF, 8])
    row_max = place("row_max", region(16), [2, HALF])
    row_sum = place("row_sum", region(16), [2, HALF])
    row_inv = place("row_inv", region(16), [2, HALF])
    at_temp = base[0]
    ada_raw = place("ada_raw", at_temp, [ADA_RING, ADA_COLS])
    ada_acc = [place("ada_acc0", at_temp + 16 * KB, [ADA_COLS]), place("ada_acc1", at_temp + 40 * KB, [ADA_COLS])]
    silu_a = place("silu_a", at_temp + 20 * KB, [HALF, NB])
    act_tok = place("act_tok", at_temp + 24 * KB, [HALF, NB])
    aT_hi = place("aT_hi", at_temp + 28 * KB, [4, T], F32R)
    aT_lo = place("aT_lo", at_temp + 32 * KB, [4, T], F32R)
    norm_tmp = place("norm_tmp", at_temp + 20 * KB, [2, 2, T])
    vecs = place("vecs", at_temp + 36 * KB, [P])
    c_row = place("c_row", at_temp + 39 * KB + 64, [P])
    convs = place("convs", at_temp + 36 * KB + 512, [P])
    badas = place("badas", at_temp + 37 * KB, [2, P])

    pos_row = place("pos_row", at_temp + 38 * KB, [T], I32)
    pos_col = place("pos_col", at_temp + 39 * KB, [HALF], I32)
    xs = place("xs", at_temp + 20 * KB, [GROUPS, HALF, T])
    front_fm = place("front_fm", at_temp + 21 * KB, [T])
    ki_tok = place("ki_tok", at_temp + 20 * KB, [HALF, 2, 64])
    zs = place("zs", at_temp + 36 * KB, [GROUPS, HALF, T])
    yT_hi = place("yT_hi", at_temp + 20 * KB, [KT, T], F32R)
    yT_lo = place("yT_lo", at_temp + 36 * KB, [KT, T], F32R)
    bT = place("bT", at_temp + 52 * KB, [GROUPS, T])
    cT = place("cT", at_temp + 60 * KB, [GROUPS, T])
    qiT = place("qiT", at_temp + 68 * KB, [IDX_H // 2, T])
    oT_hi = place("oT_hi", at_temp + 52 * KB, [KT, T], F32R)
    oT_lo = place("oT_lo", at_temp + 68 * KB, [KT, T], F32R)
    PADW = T + 4
    padded = place("padded", at_y, [2, 4, PADW])
    conv = place("conv", at_y + 9 * KB, [4, T])
    decay = place("decay", at_y, [3, 4, P])
    cb = place("cb", at_y + 6 * KB, [3, P])
    xdt = place("xdt", at_y + 8 * KB, [HALF, 4, 64])
    yg = place("yg", at_y + 10 * KB, [HALF, T])
    yg2 = place("yg2", at_y + 12 * KB, [HALF, T])
    qT = place("qT", at_y, [4, T])
    probs = place("probs", at_y + 4 * KB, [2, HALF, T])
    pT = place("pT", at_y + 8 * KB, [2, 2, T])
    sg0 = place("sg0", at_h, [HALF, NB])
    sg1 = place("sg1", at_h + 4 * KB, [HALF, NB])
    kT = place("kT", at_h + 8 * KB, [KVH, T])
    vt = place("vt", at_h + 12 * KB, [HALF, NB])
    qn = place("qn", at_temp, [HALF, NB])
    sq = place("sq", at_temp + 4 * KB, [HALF, NB])
    dist = place("dist", at_temp + 8 * KB, [HALF, T])
    score = place("score", at_temp + 10 * KB, [HALF, T])
    banned = place("banned", at_temp + 12 * KB, [HALF, T])
    rel = place("rel", at_temp + 14 * KB, [2, HALF, T])
    mT_hi = place("mT_hi", at_temp, [4, T], F32R)
    mT_lo = place("mT_lo", at_temp + 4 * KB, [4, T], F32R)
    h_dram = nc.dram_tensor("h_spill", (P, HALF, D), F32).ap()

    psum = ctx.enter_context(nc.psum_tensor("psum", [P, 8, NB], F32))

    def sem(name):
        return ctx.enter_context(nc.semaphore(name))

    raw_in = [sem(f"raw_in{k}") for k in range(RAW)]
    hi_ready = sem("hi_ready")
    split_ready = sem("split_ready")
    unit_done = sem("unit_done")
    ada_in = [sem(f"ada_in{k}") for k in range(ADA_RING)]
    ada_used = sem("ada_used")
    ada_summed = sem("ada_summed")
    mod_ready = sem("mod_ready")
    rows_in = sem("rows_in")
    c_in = sem("c_in")
    c_turned = sem("c_turned")
    c_ready = sem("c_ready")
    x_in = sem("x_in")
    consts = sem("consts")
    rows_turned = sem("rows_turned")
    cols_ready = sem("cols_ready")
    cact_ready = sem("cact_ready")
    squares = sem("squares")
    sums_ready = sem("sums_ready")
    staged = sem("staged")
    row_ready = sem("row_ready")
    mean_ready = sem("mean_ready")
    rstd_ready = sem("rstd_ready")
    xn_ready = sem("xn_ready")
    scale_ready = sem("scale_ready")
    xn_turned = sem("xn_turned")
    xm_ready = sem("xm_ready")
    xhi_ready = sem("xhi_ready")
    xlo_ready = sem("xlo_ready")
    silu_ready = sem("silu_ready")
    prod_ready = sem("prod_ready")
    act_turned = sem("act_turned")
    ahi_ready = sem("ahi_ready")
    alo_ready = sem("alo_ready")
    y_added = sem("y_added")
    y_zero = sem("y_zero")
    gate_ready = sem("gate_ready")
    gated = sem("gated")
    h_ready = sem("h_ready")
    stored = sem("stored")
    pair_read = [sem("pair_read0"), sem("pair_read1")]
    pos_in = sem("pos_in")
    pos_ready = sem("pos_ready")
    q_scale_ready = sem("q_scale_ready")
    h_spilled = sem("h_spilled")
    h_loaded = sem("h_loaded")
    pads = sem("pads")
    taps = sem("taps")
    conv_out = sem("conv_out")
    xs_turned = sem("xs_turned")
    xs_ready = sem("xs_ready")
    front_in = [sem("front_in0"), sem("front_in1")]
    front_copied = sem("front_copied")
    front_turned = sem("front_turned")
    front_read = sem("front_read")
    ki_turned = sem("ki_turned")
    kiT_ready = sem("kiT_ready")
    dt_step = sem("dt_step")
    dt_exp = sem("dt_exp")
    a_exp_ready = sem("a_exp_ready")
    dta_ready = sem("dta_ready")
    cum_ready = sem("cum_ready")
    acum_ready = sem("acum_ready")
    cb_ready = sem("cb_ready")
    seg_ready = sem("seg_ready")
    decay_ready = sem("decay_ready")
    masked_ready = sem("masked_ready")
    y_raw = sem("y_raw")
    y_step = sem("y_step")
    y_gated = sem("y_gated")
    y_squares = sem("y_squares")
    y_rstd_ready = sem("y_rstd_ready")
    y_normed = sem("y_normed")
    y_turned = sem("y_turned")
    y_hi = sem("y_hi")
    y_lo = sem("y_lo")
    index_done = sem("index_done")
    rel_ready = sem("rel_ready")
    score_step = sem("score_step")
    top_step = sem("top_step")
    dist_ready = sem("dist_ready")
    sq_ready = sem("sq_ready")
    head_sums = sem("head_sums")
    head_rstd = sem("head_rstd")
    head_turned = sem("head_turned")
    head_ready = sem("head_ready")
    logits_done = sem("logits_done")
    logit_step = sem("logit_step")
    logits_ready = sem("logits_ready")
    exp_done = sem("exp_done")
    inv_ready = sem("inv_ready")
    probs_ready = sem("probs_ready")
    probs_turned = sem("probs_turned")
    pT_ready = sem("pT_ready")
    o_done = sem("o_done")
    o_hi = sem("o_hi")
    o_lo = sem("o_lo")
    merge_step = sem("merge_step")
    merged = sem("merged")
    merged_turned = sem("merged_turned")
    m_hi = sem("m_hi")
    m_lo = sem("m_lo")

    FFN_UNITS = FBLK * 3 * UPB
    WBLOCKS = ([("b", i, B0 + i * NB) for i in range(2)] + [("c", i, C0 + i * NB) for i in range(2)]
               + [("xs", i, XS0 + i * NB) for i in range(4)] + [("z", i, Z0 + i * NB) for i in range(4)]
               + [("qi", i, QI0 + i * NB) for i in range(2)] + [("k", 0, K0), ("v", 0, V0)]
               + [("q", i, Q0 + i * NB) for i in range(4)])
    NW = len(WBLOCKS)
    MIX = FFN_UNITS
    FRONT = MIX + UPB
    FRONT_COLS = SSD_H + G0 - KI0
    FRONT_KT = KT // 2
    FRONT_UNITS = range(FRONT, FRONT + 2)
    FRONT_END = FRONT + 2
    start = [MIX] + [FRONT_END + UPB * b for b in range(NW - 1)]
    end = [s + UPB for s in start]
    M0 = end[-1]
    M1 = M0 + 4 * UPB
    MBODY = 5 * UPB
    MEND = M1 + (QB - 1) * MBODY
    kind = [w[0] for w in WBLOCKS]
    at_block = {k: kind.index(k) for k in ("b", "c", "xs", "z", "qi", "k", "v", "q")}
    ssd_start = [start[at_block["z"] + 1 + g] for g in range(GROUPS)]
    index_slot = ([start[at_block["k"]] + 3 + j for j in range(4)] + [start[at_block["v"]] + 3 + j for j in range(4)])
    att_start = [start[at_block["q"] + 2], start[at_block["q"] + 3], M0, M0 + UPB]
    att_slot = [att_start[a // 4] + 2 * (a % 4) for a in range(HEADS)]
    ffn_base = [0, MEND + UPB]
    Y_ADDS = [0, (FBLK + QB) * QB]
    Y_MIX = FBLK * QB
    ffn_w = [(ffn1_w1[0], ffn1_w3[0], ffn1_w2[0]), (ffn2_w1[0], ffn2_w3[0], ffn2_w2[0])]
    ffn_norm_col = [16, 48]
    FIRST = 2 * UPB
    BLOCK = 3 * UPB
    PEELED = FIRST + 2 * BLOCK
    BODY = 2 * BLOCK
    mod_cols = lambda chunk: slice(chunk * KT, (chunk + 1) * KT)

    def rows_cols(w, row, cols):
        return w[row:row + 2 * P, cols].rearrange("(k p) n -> p k n", p=P)

    def span(start, size):
        return slice(start, start + size) if isinstance(start, int) else bass.ds(start, size)

    def ffn_sources(f, first, i):
        w1, w3, w2 = ffn_w[f]
        if first:
            cols = slice(0, NB)
            return ([rows_cols(w1, 2 * P * u, cols) for u in range(UPB)]
                    + [rows_cols(w3, 2 * P * u, cols) for u in range(UPB)])
        w2_rows = w2[span(i * NB, NB), :]
        cols = span((i + 1) * NB, NB)
        return ([rows_cols(w1, 2 * P * u, cols) for u in range(UPB)] + ffn_w2_sources(w2_rows)
                + [rows_cols(w3, 2 * P * u, cols) for u in range(UPB)])

    def ffn_w2_sources(w2_rows):
        return [rows_cols(w2_rows, 2 * P * k, slice(q * NB, (q + 1) * NB)) for q in range(QB) for k in range(2)]

    def mix_source(n):
        b = max(i for i in range(NW) if start[i] <= n)
        return rows_cols(w_in[0], 2 * P * (n - start[b]), slice(WBLOCKS[b][2], WBLOCKS[b][2] + NB))

    def block_sources(w, cols):
        return [rows_cols(w, 2 * P * u, cols) for u in range(UPB)]

    def merge_sources(b, trip):
        sl = (lambda base: slice(base, base + NB)) if b == 0 else (lambda base: bass.ds(trip * NB + (base + NB), NB))
        parts = block_sources(w_in[0], sl(G0)) + block_sources(w_in[0], sl(G0 + D))
        if b:
            parts += ffn_w2_sources(w_out[0][bass.ds(trip * NB, NB), :])
        return parts + block_sources(w_br_ssd[0], sl(0)) + block_sources(w_br_att[0], sl(0))


    def ada_source(e, k):
        return w_ada[0][k * P:(k + 1) * P, span(e * ADA_COLS, ADA_COLS)]

    def ada_slot(m):
        merge, ffn2 = ADA_MERGE * KT, ADA_FFN2 * KT
        if m.n0 < merge:
            return m.n0 % ADA_RING, m.count(each=ADA_RING, plus=1), m.count(plus=1 - ADA_RING) if m.n0 >= ADA_RING else None
        if m.n0 < ffn2:
            return 2 + m.n0 % 2, (m + -merge).count(each=2, plus=merge // ADA_RING + 1), m.count(plus=-1)
        slot = m.n0 % ADA_RING
        before = merge // ADA_RING + ((ffn2 - merge) // 2 if slot >= 2 else 0)
        return slot, (m + -ffn2).count(each=ADA_RING, plus=before + 1), max(m.n0 + 1 - ADA_RING, ffn2)

    def ada_at(i):
        return 4 + i * 13 // 8

    def ada_unit_after(where, w):
        if where == "peeled":
            at = [ada_at(i) for i in range(ADA_PEELED * KT)]
        elif where == "trip":
            at = [6 + 2 * i for i in range(KT)]
        else:
            at = [1 + 2 * i for i in range(KT)]
        return at.index(w) if w in at else None

    ADA_SUM_AT = 2 * UPB + 4
    def turn_bank(f, j):
        if f == 0:
            return 2 + j % 2
        return 0 if j < 2 else (j + 1) % 2

    as2 = lambda t: t.rearrange("p (k n) -> p k n", k=2)

    block = ctx.enter_context(nc.Block())

    @block.sync
    def _(sp):
        def load_unit(n, source):
            s = n.slot(RAW)
            if n.n0 >= RAW:
                sp.wait_ge(split_ready, n.count(plus=1 - RAW))
            sp.dma_start(as2(raw[:, s, :]), source).then_inc(raw_in[s], 16)

        def load_ada(m, source):
            slot, _, free = ada_slot(m)
            if free is not None:
                sp.wait_ge(ada_used, free)
            sp.dma_start(ada_raw[:, slot, :], source).then_inc(ada_in[slot], 16)

        for e in range(ADA_FIRST):
            for k in range(KT):
                load_ada(At(e * KT + k), ada_source(e, k))
                if e == 0 and k == ADA_RING - 1:
                    for u, source in enumerate(ffn_sources(0, True, 0)[0:RAW]):
                        load_unit(At(u), source)
            if e == 0:
                sp.dma_start(h[:], x[0].rearrange("(s p) d -> p s d", p=P)).then_inc(x_in, 16)
        for f in range(2):
            n = ffn_base[f]
            peeled = ffn_sources(f, True, 0) + ffn_sources(f, False, 0) + ffn_sources(f, False, 1)
            for u, source in enumerate(peeled):
                if f or u >= RAW:
                    load_unit(At(n + u), source)
                i = ada_unit_after("peeled", u)
                if i is not None:
                    e, k = divmod(i, KT)
                    e += (ADA_FIRST, ADA_FFN2)[f]
                    if f and i == 0:
                        sp.wait_ge(unit_done, n)
                    load_ada(At(e * KT + k), ada_source(e, k))
            with sp.Fori(0, TRIPS) as trip:
                pair_of_blocks = ffn_sources(f, False, trip * 2 + 2) + ffn_sources(f, False, trip * 2 + 3)
                for u, source in enumerate(pair_of_blocks):
                    load_unit(At(n + PEELED + u, BODY, trip), source)
                    k = ada_unit_after("trip", u)
                    if f == 0 and k is not None:
                        e = ADA_FIRST + ADA_PEELED
                        load_ada(At(e * KT + k, KT, trip), ada_source(trip + e, k))
            for u, source in enumerate(ffn_w2_sources(ffn_w[f][2][(FBLK - 1) * NB:, :])):
                load_unit(At(n + FFN_UNITS - UPB + u), source)
            if f == 1:
                break
            mix_ada = ADA_MIX * KT
            for n in range(MIX, M0):
                if n in FRONT_UNITS:
                    s = At(n).slot(RAW)
                    rows = slice((n - FRONT) * FRONT_KT * P, (n - FRONT + 1) * FRONT_KT * P)
                    dst = raw[:, s, 0:FRONT_KT * FRONT_COLS].rearrange("p (k n) -> p k n", k=FRONT_KT)
                    sp.wait_ge(split_ready, n + 1 - RAW)
                    sp.dma_start(dst[:, :, 0:SSD_H],
                                 w_in[0][rows, DT0:DT0 + SSD_H].rearrange("(k p) n -> p k n", p=P)).then_inc(front_in[n - FRONT], 16)
                    sp.dma_start(dst[:, :, SSD_H:],
                                 w_in[0][rows, KI0:G0].rearrange("(k p) n -> p k n", p=P)).then_inc(raw_in[s], 16)
                    continue
                load_unit(At(n), mix_source(n))
                if n < start[at_block["qi"]] and (n - (MIX if n < FRONT else FRONT_END)) % 2:
                    load_ada(At(mix_ada), ada_source(mix_ada // KT, mix_ada % KT))
                    mix_ada += 1
            for u, source in enumerate(merge_sources(0, 0)):
                load_unit(At(M0 + u), source)
            sp.wait_ge(logits_ready, HEADS)
            with sp.Fori(0, QB - 1) as trip:
                for u, source in enumerate(merge_sources(1, trip)):
                    load_unit(At(M1 + u, MBODY, trip), source)
                    k = ada_unit_after("merge", u)
                    if k is not None:
                        load_ada(At(ADA_MERGE * KT + k, KT, trip), ada_source(trip + ADA_MERGE, k))
            for u, source in enumerate(ffn_w2_sources(w_out[0][(QB - 1) * NB:, :])):
                load_unit(At(MEND + u), source)
        for q in range(QB):
            cols = slice(q * NB, (q + 1) * NB)
            sp.wait_ge(h_ready, 2 * QB + q + 1)
            sp.dma_start(out[0].rearrange("(s p) d -> p s d", p=P)[:, :, cols], h[:, :, cols]).then_inc(stored, 16)
        sp.wait_ge(stored, 16 * QB)

    @block.gpsimd
    def _(pool):
        nc.gpsimd.memset(ident[:], 0.0).then_inc(consts, 1)
        nc.gpsimd.memset(upper[:], 1.0).then_inc(consts, 1)
        nc.gpsimd.memset(ones[:], 1.0).then_inc(consts, 1)
        nc.gpsimd.memset(mhalf[:], -0.5).then_inc(consts, 1)
        pool.wait_ge(consts, 4)
        nc.gpsimd.affine_select(out=ident[:], in_=ident[:], compare_op=ALU.not_equal, fill=1.0, base=0,
                                pattern=[[1, P]], channel_multiplier=-1).then_inc(consts, 1)
        nc.gpsimd.affine_select(out=upper[:], in_=upper[:], compare_op=ALU.is_ge, fill=0.0, base=0,
                                pattern=[[1, P]], channel_multiplier=-1).then_inc(consts, 1)

        means = [0]

        def inverse_root(dst, mid, src, size, signal):
            nc.gpsimd.tensor_scalar(mid, src, 1.0 / size, EPS, ALU.mult, ALU.add).then_inc(mean_ready, 1)
            means[0] += 1
            pool.wait_ge(mean_ready, means[0])
            nc.gpsimd.tensor_tensor(dst, mid, mhalf[:, 0:src.shape[-1]], ALU.pow).then_inc(signal, 1)

        def norm(f):
            pool.wait_ge(sums_ready, f + 1)
            inverse_root(rstd[:], rbase[:], row_sums[:], D, rstd_ready)

        norm(0)
        pool.wait_ge(xn_turned, UPB)
        nc.gpsimd.memset(y[:], 0.0).then_inc(y_zero, 1)
        norm(1)
        pool.wait_ge(squares, 2 * QB)
        nc.gpsimd.memset(padded[:, :, :, 0:3], 0.0).then_inc(pads, 1)
        for n in range(MIX, M1):
            for g in range(GROUPS):
                if n == ssd_start[g] + 9:
                    pool.wait_ge(y_squares, g + 1)
                    inverse_root(y_rstd[:], y_base[:], y_sum[:], T, y_rstd_ready)
            for i, b in enumerate([at_block["k"]] + [at_block["q"] + j for j in range(4)]):
                if n == end[b] + 3:
                    pool.wait_ge(head_sums, i + 1)
                    inverse_root(h_rstd[:], h_base[:], h_sum[:], HD, head_rstd)
        norm(2)
        pool.wait_ge(squares, 3 * QB)
        nc.gpsimd.memset(y[:], 0.0).then_inc(y_zero, 1)

    @block.scalar
    def _(act):
        done = [0]

        def rows(dst, src):
            act.dma_start(dst, src).then_inc(rows_in, 16)

        act.dma_start(c_row[0:KT, :], c[0].rearrange("(r n) -> r n", n=P)).then_inc(c_in, 16)
        row = 0
        for v, count in ((c, 16), (norm_ffn1, 16), (norm_mix, 16), (norm_ffn2, 16), (ssd_norm, 16),
                         (ssd_conv_b, 32), (q_norm, 1), (k_norm, 1)):
            rows(vecs[row:row + count, :], v[0].rearrange("(r n) -> r n", n=P))
            row += count
        rows(convs[:], ssd_conv_w[0].rearrange("j (r n) -> (j r) n", n=P))
        rows(badas[:, 0, :], b_ada[0][0:P * P].rearrange("(r n) -> r n", n=P))
        rows(badas[0:16, 1, :], b_ada[0][P * P:].rearrange("(r n) -> r n", n=P))
        def spread(dst, src):
            act.dma_start(dst, src.rearrange("(o n) -> o n", o=1).broadcast_to((P, src.shape[0]))).then_inc(pos_in, 16)

        spread(dt_bias[:], ssd_dt_bias[0])
        spread(a_exp[:], ssd_a_log[0])
        spread(skip[:], ssd_d[0])
        spread(pos_row[:], positions[0])
        act.dma_start(pos_col[:], positions[0].rearrange("(s p) -> p s", p=P),
                      allow_slow_non_contiguous=True).then_inc(pos_in, 16)

        def cast_units(upto):
            while done[0] < upto:
                cast(At(done[0]))
                done[0] += 1

        def cast(n):
            act.wait_ge(raw_in[n.slot(RAW)], n.count(each=RAW, plus=1) * 16)
            if n.n0 >= SPLIT:
                act.wait_ge(unit_done, n.count(plus=1 - SPLIT))
            size = UNIT
            if n.per == 0 and n.n0 in FRONT_UNITS:
                act.wait_ge(front_in[n.n0 - FRONT], 16)
                size = FRONT_KT * FRONT_COLS
            nc.scalar.activation(w_hi[:, n.slot(SPLIT), 0:size], raw[:, n.slot(RAW), 0:size], ACT.Copy).then_inc(hi_ready, 1)

        act.wait_ge(c_ready, 1)
        nc.scalar.activation(cact[:], vecT[:, 0:KT], ACT.Silu).then_inc(cact_ready, 1)
        act.wait_ge(pos_in, 16 * 5)
        nc.scalar.activation(a_exp[:], a_exp[:], ACT.Exp).then_inc(a_exp_ready, 1)

        def square(f, q):
            cols = slice(q * NB, (q + 1) * NB)
            for half in range(HALF):
                ins = nc.scalar.activation(y[:, half, cols], h[:, half, cols], ACT.Square,
                                           accum_out=ssum[:, half, q:q + 1])
            ins.then_inc(squares, 1)

        def stage(f, j):
            act.wait_ge(xn_turned, UPB * f + j + 1)
            bank = turn_bank(f, j)
            if f == 0:
                ins = nc.scalar.activation(xT_raw[:, 2 * j:2 * j + 2, :], psum[:, bank, :].rearrange("p (k t) -> p k t", k=2), ACT.Copy)
            else:
                for k in range(2):
                    ins = nc.scalar.activation(xT_raw[:, 2 * j + k, :], psum[:, bank, k * T:(k + 1) * T], ACT.Copy,
                                               scale=scale_col[:, 2 * j + k:2 * j + k + 1])
            ins.then_inc(staged, 1)

        def norm_first():
            act.wait_ge(x_in, 16)
            for q in range(QB):
                square(0, q)
            act.wait_ge(rstd_ready, 1)
            for half in range(HALF):
                nc.scalar.activation(y[:, half, :], h[:, half, :], ACT.Copy, scale=rstd[:, half:half + 1]).then_inc(xn_ready, 1)
            for j in range(UPB):
                stage(0, j)
            cast_units(SPLIT)

        def turn_tail(f, n):
            for q in range(QB):
                cast_units(n + 2 * q + 5)
                act.wait_ge(h_ready, (f - 1) * QB + q + 1)
                square(f, q)
                if f == 1 and q == QB - 1:
                    act.dma_start(h_dram, h[:]).then_inc(h_spilled, 16)
                if q == 0:
                    act.wait_ge(scale_ready, f + 1)
                stage(f, 2 * q)
                cast_units(n + 2 * q + 6)
                stage(f, 2 * q + 1)

        def norm(f):
            for j in range(UPB):
                act.wait_ge(xm_ready, UPB * f + j + 1)
                if f == 0:
                    ins = nc.scalar.activation(xT_hi[:, 2 * j:2 * j + 2, :], norm_tmp[:, j % 2], ACT.Copy)
                else:
                    for k in range(2):
                        col = mod_cols((0, 3, 6)[f]).start + 2 * j + k
                        ins = nc.scalar.activation(xT_hi[:, 2 * j + k, :], norm_tmp[:, j % 2, k, :], ACT.Identity,
                                                   bias=modT[:, col:col + 1])
                ins.then_inc(xhi_ready, 1)
                if j:
                    cast_units((0, MIX, ffn_base[1])[f] + j + 2)

        def silu(o):
            act.wait_ge(prod_ready, o.count()) if o.n0 else None
            for s in range(HALF):
                ins = nc.scalar.activation(silu_a[:, s, :], psum[:, s, :], ACT.Silu)
            ins.then_inc(silu_ready, 1)

        def act_hi(o):
            act.wait_ge(act_turned, o.count(plus=1))
            for j in range(2):
                ins = nc.scalar.activation(aT_hi[:, 2 * j:2 * j + 2, :], psum[:, 4 + j, :].rearrange("p (k t) -> p k t", k=2), ACT.Copy)
            ins.then_inc(ahi_ready, 1)

        def ffn(f):
            n0 = ffn_base[f]
            o0 = f * FBLK
            cast_units(n0 + UPB + LAG)
            act.wait_ge(unit_done, n0 + UPB)
            silu(At(o0))
            cast_units(n0 + FIRST)

            def hidden(n, o):
                for u in range(BLOCK):
                    if n.per:
                        cast(n + u)
                    else:
                        cast_units(n.n0 + u + 1)
                    if u == 7:
                        act_hi(o)
                    if u == UPB - 1 + LAG:
                        act.wait_ge(unit_done, (n + UPB).count())
                        silu(o + 1)

            for e in range(2):
                hidden(At(n0 + FIRST + e * BLOCK), At(o0 + e))
            with act.Fori(0, TRIPS) as trip:
                for e in range(2):
                    hidden(At(n0 + PEELED + e * BLOCK, BODY, trip), At(o0 + 2 + e, 2, trip))
            done[0] = n0 + FFN_UNITS - UPB
            cast_units(n0 + FFN_UNITS - UPB + LAG)
            act_hi(At(o0 + FBLK - 1))
            if f == 0:
                turn_tail(1, n0 + FFN_UNITS - UPB)
            cast_units(n0 + FFN_UNITS + (SPLIT if f == 0 else 0))

        def pair(b):
            return 2 * (b % 2)

        def conv_in(b):
            act.wait_ge(unit_done, end[b])
            act.wait_ge(pads, 1)
            if b >= 2:
                act.wait_ge(taps, 12 * (b - 1))
            if b >= 1:
                act.wait_ge(conv_out, b)
            if b > at_block["xs"]:
                act.wait_ge(xs_turned, b - at_block["xs"])
            for j in range(2):
                src = psum[:, pair(b) + j, :].rearrange("p (k t) -> p k t", k=2)
                nc.scalar.activation(padded[:, b % 2, 2 * j:2 * j + 2, 3:3 + T], src, ACT.Copy)
            channel = {"xs": 0, "b": 16, "c": 24}[kind[b]] + 4 * WBLOCKS[b][1]
            for k in range(4):
                ins = nc.scalar.activation(conv[:, k, :], psum[:, pair(b) + k // 2, (k % 2) * T:(k % 2 + 1) * T],
                                           ACT.Identity, scale=convT[:, 96 + channel + k:97 + channel + k],
                                           bias=vecT[:, 80 + channel + k:81 + channel + k])
            ins.then_inc(pair_read[b % 2], 1)

        def conv_silu(b):
            act.wait_ge(taps, 12 * (b + 1))
            i = WBLOCKS[b][1]
            dst = {"xs": conv, "b": bT, "c": cT}[kind[b]]
            first = 0 if kind[b] == "xs" else 4 * i
            nc.scalar.activation(dst[:, first:first + 4, :], conv[:], ACT.Silu).then_inc(conv_out, 1)

        def by_group(bank):
            return psum[:, bank, :].rearrange("p (g n) -> p g n", g=2)

        def xs_out(b):
            i = WBLOCKS[b][1]
            act.wait_ge(xs_turned, i + 1)
            for half in range(HALF):
                ins = nc.scalar.activation(xs[:, 2 * i:2 * i + 2, half, :], by_group(4 + half), ACT.Copy)
            ins.then_inc(xs_ready, 1)

        def z_out(b):
            i = WBLOCKS[b][1]
            act.wait_ge(unit_done, end[b])
            for half in range(HALF):
                ins = nc.scalar.activation(zs[:, 2 * i:2 * i + 2, half, :], by_group(pair(b) + half), ACT.Silu)
            ins.then_inc(pair_read[b % 2], 1)

        def front_copy():
            act.wait_ge(unit_done, FRONT_END)
            nc.scalar.activation(front_fm[0:FRONT_COLS, :], psum[0:FRONT_COLS, 5, 0:T], ACT.Copy).then_inc(front_copied, 1)

        def front_out():
            act.wait_ge(front_turned, 1)
            act.wait_ge(dt_step, 2)
            key_weight = psum[:, 4, 0:2 * FRONT_COLS].rearrange("p (s n) -> p s n", s=2)[:, :, SSD_H:]
            nc.scalar.activation(wi[:], key_weight[:, :, 64:80], ACT.Copy, scale=float((64 * IDX_H) ** -0.5))
            for e in range(2):
                ins = nc.scalar.activation(ki_tok[:, :, e, :], key_weight[:, :, 0:64], ACT.Copy)
            ins.then_inc(front_read, 1)
            nc.scalar.activation(sp_e[:], sp_e[:], ACT.Exp, scale=-1.0).then_inc(dt_exp, 1)

        def kiT_out():
            act.wait_ge(ki_turned, 1)
            nc.scalar.activation(kiT[:], psum[:, 5, 0:T], ACT.Copy).then_inc(kiT_ready, 1)

        def qi_out(b):
            i = WBLOCKS[b][1]
            act.wait_ge(unit_done, end[b])
            for j in range(2):
                ins = nc.scalar.activation(qiT[:, 4 * i + 2 * j:4 * i + 2 * j + 2, :],
                                           psum[:, pair(b) + j, :].rearrange("p (k t) -> p k t", k=2), ACT.Copy)
            ins.then_inc(pair_read[b % 2], 1)

        def v_out(b):
            act.wait_ge(unit_done, end[b])
            act.wait_ge(h_spilled, 16)
            for half in range(HALF):
                ins = nc.scalar.activation(vt[:, half, :], psum[:, pair(b) + half, :], ACT.Copy)
            ins.then_inc(pair_read[b % 2], 1)

        def head_squares(i, b):
            act.wait_ge(unit_done, end[b])
            if i:
                act.wait_ge(head_sums, i)
            for half in range(HALF):
                ins = nc.scalar.activation(sq[:, half, :], psum[:, pair(b) + half, :], ACT.Square)
            ins.then_inc(sq_ready, 1)

        def k_out():
            act.wait_ge(head_turned, 1)
            act.wait_ge(h_spilled, 16)
            for j in range(2):
                ins = nc.scalar.activation(kT[:, 2 * j:2 * j + 2, :], psum[:, 5 + j, :].rearrange("p (k t) -> p k t", k=2),
                                           ACT.Copy, scale=vecT[:, 113:114])
            ins.then_inc(head_ready, 1)

        def q_out(i, j):
            act.wait_ge(head_turned, 1 + 2 * i + j + 1)
            act.wait_ge(q_scale_ready, 1)
            nc.scalar.activation(qT[:, 2 * j:2 * j + 2, :], psum[:, 7, :].rearrange("p (k t) -> p k t", k=2),
                                 ACT.Copy, scale=q_scale[:, 0:1]).then_inc(head_ready, 1)

        def index_relu(j):
            act.wait_ge(index_done, j + 1)
            if j:
                act.wait_ge(score_step, 4 * j)
            for e in range(2):
                ins = nc.scalar.activation(rel[:, e], psum[:, 5 + e, :].rearrange("p (s t) -> p s t", s=2), ACT.Relu)
            ins.then_inc(rel_ready, 1)

        def decay_exp(g):
            act.wait_ge(seg_ready, g + 1)
            nc.scalar.activation(decay[:], decay[:], ACT.Exp).then_inc(decay_ready, 1)

        def y_square(g):
            act.wait_ge(y_gated, g + 1)
            for half in range(HALF):
                ins = nc.scalar.activation(yg2[:, half, :], yg[:, half, :], ACT.Square, accum_out=y_sum[:, half:half + 1])
            ins.then_inc(y_squares, 1)

        def y_hi_out(g):
            act.wait_ge(y_turned, g + 1)
            for k in range(2):
                ins = nc.scalar.activation(yT_hi[:, 2 * g + k, :], psum[:, 4, k * T:(k + 1) * T], ACT.Copy,
                                           scale=vecT[:, 64 + 2 * g + k:65 + 2 * g + k])
            ins.then_inc(y_hi, 1)

        def probs_exp(a):
            act.wait_ge(logits_ready, a + 1)
            for half in range(HALF):
                ins = nc.scalar.activation(probs[:, a % 2, half, :], probs[:, a % 2, half, :], ACT.Exp,
                                           bias=row_max[:, a % 2, half:half + 1],
                                           accum_out=row_sum[:, a % 2, half:half + 1])
            ins.then_inc(exp_done, 1)

        def probs_out(a):
            act.wait_ge(probs_turned, a + 1)
            if a >= 2:
                act.wait_ge(o_done, a - 1)
            nc.scalar.activation(pT[:, a % 2], psum[:, 6, :].rearrange("p (k t) -> p k t", k=2),
                                 ACT.Copy).then_inc(pT_ready, 1)

        def o_hi_out(a):
            act.wait_ge(o_done, a + 1)
            nc.scalar.activation(oT_hi[:, a, :], psum[:, 4, 0:T], ACT.Copy).then_inc(o_hi, 1)

        def gate_out(n, b, which):
            act.wait_ge(unit_done, n.count())
            if b.n0:
                act.wait_ge(merged_turned, b.count())
            dst = (sg0, sg1)[which]
            for half in range(HALF):
                ins = nc.scalar.activation(dst[:, half, :], psum[:, 2 * which + half, :], ACT.Sigmoid)
            ins.then_inc(pair_read[which], 1)

        def merged_hi(b):
            act.wait_ge(merged_turned, b.count(plus=1))
            for j in range(2):
                ins = nc.scalar.activation(mT_hi[:, 2 * j:2 * j + 2, :], psum[:, 4 + j, :].rearrange("p (k t) -> p k t", k=2), ACT.Copy)
            ins.then_inc(m_hi, 1)

        def mixer():
            for n in range(MIX, M1):
                cast_units(n + 1)
                for b in range(NW):
                    if kind[b] in ("b", "c", "xs"):
                        if n == end[b] + 2:
                            conv_in(b)
                        if n == end[b] + 6:
                            conv_silu(b)
                        if kind[b] == "xs" and n == end[b] + 9:
                            xs_out(b)
                    if n == end[b] + 2:
                        if kind[b] == "z":
                            z_out(b)
                        if kind[b] == "qi":
                            qi_out(b)
                        if kind[b] == "v":
                            v_out(b)
                        if kind[b] == "k":
                            head_squares(0, b)
                        if kind[b] == "q":
                            head_squares(1 + WBLOCKS[b][1], b)
                    if kind[b] == "k" and n == end[b] + 9:
                        k_out()
                    if kind[b] == "q" and n in (end[b] + 7, end[b] + 9):
                        q_out(WBLOCKS[b][1], (n - end[b] - 7) // 2)
                if n == FRONT_END + 2:
                    front_copy()
                if n == FRONT_END + 6:
                    front_out()
                if n == FRONT_END + 11:
                    kiT_out()
                for g in range(GROUPS):
                    s = ssd_start[g]
                    if n == s + 3:
                        decay_exp(g)
                    if n == s + 8:
                        y_square(g)
                    if n == s + 12:
                        y_hi_out(g)
                for j in range(8):
                    if n == index_slot[j] + 2:
                        index_relu(j)
                for a in range(HEADS):
                    if n == att_slot[a] + 3:
                        probs_exp(a)
                    if n == att_slot[a] + 6:
                        probs_out(a)
                    if n == att_slot[a] + 9:
                        o_hi_out(a)
                if n == M0 + 10:
                    gate_out(At(M0 + UPB), At(0), 0)
                if n == M0 + 18:
                    gate_out(At(M0 + 2 * UPB), At(0), 1)
            with act.Fori(0, QB - 1) as trip:
                m = At(M1, MBODY, trip)
                b = At(1, 1, trip)
                for u in range(MBODY):
                    cast(m + u)
                    if u == 7:
                        merged_hi(At(0, 1, trip))
                    if u == 10:
                        gate_out(m + UPB, b, 0)
                    if u == 18:
                        gate_out(m + 2 * UPB, b, 1)
            done[0] = MEND
            cast_units(MEND + SPLIT - 1)
            merged_hi(At(QB - 1))
            act.wait_ge(merged_turned, QB)
            act.dma_start(h[:], h_dram).then_inc(h_loaded, 16)
            turn_tail(2, MEND)

        norm_first()
        norm(0)
        ffn(0)
        norm(1)
        mixer()
        norm(2)
        ffn(1)

    @block.vector
    def _(dve):
        done = [0]

        def sub(n):
            dve.wait_ge(hi_ready, n.count(plus=1))
            size = FRONT_KT * FRONT_COLS if n.per == 0 and n.n0 in FRONT_UNITS else UNIT
            nc.vector.tensor_tensor(w_lo[:, n.slot(SPLIT), 0:size], raw[:, n.slot(RAW), 0:size],
                                    w_hi[:, n.slot(SPLIT), 0:size], ALU.subtract).then_inc(split_ready, 1)

        def sub_units(upto):
            while done[0] < upto:
                sub(At(done[0]))
                done[0] += 1

        def ada_acc_of(e):
            if e.per == 0 and (e.n0 < ADA_FIRST + ADA_PEELED or e.n0 >= ADA_FFN2):
                return ada_acc[e.n0 % 2], True
            return ada_acc[0], False

        def ada_add(m, k):
            slot, landed, _ = ada_slot(m)
            e = At(m.n0 // KT, m.per // KT, m.trip)
            acc, two = ada_acc_of(e)
            dve.wait_ge(ada_in[slot], landed * 16)
            src = ada_raw[:, slot, :]
            if k == 0:
                if e.n0 >= (2 if two else 1):
                    dve.wait_ge(ada_summed, e.count(plus=-1 if two else 0))
                nc.vector.tensor_scalar(acc[:], src, cact[:, 0:1], None, ALU.mult).then_inc(ada_used, 1)
            else:
                dve.wait_ge(ada_used, m.count())
                nc.vector.scalar_tensor_tensor(out=acc[:], in0=src, scalar=cact[:, k:k + 1], in1=acc[:],
                                               op0=ALU.mult, op1=ALU.add).then_inc(ada_used, 1)

        def mod_out(e, bank):
            cols = bass.ds(e.count() * 8, 8) if e.per else slice(e.n0 * 8, e.n0 * 8 + 8)
            dve.wait_ge(ada_summed, e.count(plus=1))
            nc.vector.tensor_tensor(modT[:, cols], psum[:, bank, 0:8], badaT[:, cols], ALU.add).then_inc(mod_ready, 1)

        dve.wait_ge(c_turned, 1)
        nc.vector.tensor_copy(vecT[:, 0:KT], psum[:, 1, 0:KT]).then_inc(c_ready, 1)

        def columns():
            dve.wait_ge(rows_turned, 1)
            nc.vector.tensor_copy(vecT[:, KT:114], psum[:, 0, KT:114])
            nc.vector.tensor_copy(convT[:], psum[:, 0, 128:256])
            nc.vector.tensor_copy(badaT[:], psum[:, 0, 256:400]).then_inc(cols_ready, 1)

        def position_rows():
            dve.wait_ge(pos_in, 16 * 5)
            dve.wait_ge(cols_ready, 1)
            nc.vector.tensor_scalar(q_scale[:], vecT[:, 112:113], float(HD ** -0.5), None, ALU.mult).then_inc(q_scale_ready, 1)
            nc.vector.tensor_copy(key_pos[:], pos_row[:])
            nc.vector.tensor_copy(query_pos[:], pos_col[:]).then_inc(pos_ready, 1)
            dve.wait_ge(pos_ready, 1)
            nc.vector.tensor_scalar(pos_row[:], pos_row[:], 6, None, ALU.arith_shift_right)
            nc.vector.tensor_scalar(pos_col[:], pos_col[:], 6, None, ALU.arith_shift_right).then_inc(pos_ready, 1)
            dve.wait_ge(pos_ready, 2)
            nc.vector.tensor_copy(key_chunk[:], pos_row[:])
            nc.vector.tensor_copy(query_chunk[:], pos_col[:]).then_inc(pos_ready, 1)

        def sum_squares(f):
            dve.wait_ge(squares, QB * (f + 1))
            nc.vector.tensor_reduce(row_sums[:], ssum[:], AX.X, ALU.add).then_inc(sums_ready, 1)

        dve.wait_ge(cact_ready, 1)
        for e in range(ADA_FIRST):
            for k in range(KT):
                ada_add(At(e * KT + k), k)
                if e == 0 and k == 8:
                    columns()
                if e == 0 and k == 12:
                    position_rows()
                if e == 1 and k == 10:
                    sum_squares(0)
                if e and k == 0:
                    mod_out(At(e - 1), 0)
        sub_units(SPLIT)
        mod_out(At(ADA_FIRST - 1), 0)

        peeled = [0, 0]

        def ada_peeled(f):
            while peeled[f] < ADA_PEELED * KT and done[0] > ffn_base[f] + ada_at(peeled[f]):
                e, k = divmod(peeled[f], KT)
                e += (ADA_FIRST, ADA_FFN2)[f]
                ada_add(At(e * KT + k), k)
                peeled[f] += 1

        def scale_out(f):
            dve.wait_ge(mod_ready, (4, 10, 16)[f])
            nc.vector.scalar_tensor_tensor(out=scale_col[:], in0=modT[:, mod_cols((1, 4, 7)[f])], scalar=1.0,
                                           in1=vecT[:, 16 * (f + 1):16 * (f + 1) + KT], op0=ALU.add,
                                           op1=ALU.mult).then_inc(scale_ready, 1)

        def norm(f):
            first = (0, MIX, ffn_base[1])[f]
            if f == 0:
                scale_out(0)
                dve.wait_ge(scale_ready, 1)
                dve.wait_ge(staged, UPB)
            else:
                sum_squares(f)
                sub_units(first + 2)
                dve.wait_ge(row_ready, f)
            shift = mod_cols((0, 3, 6)[f]).start

            def lo(j):
                dve.wait_ge(xhi_ready, UPB * f + j + 1)
                if f == 0:
                    ins = nc.vector.tensor_tensor(xT_lo[:, 2 * j:2 * j + 2, :], norm_tmp[:, j % 2], xT_hi[:, 2 * j:2 * j + 2, :],
                                                  ALU.subtract)
                else:
                    for k in range(2):
                        col = 2 * j + k
                        ins = nc.vector.scalar_tensor_tensor(out=xT_lo[:, col, :], in0=norm_tmp[:, j % 2, k, :],
                                                             scalar=modT[:, shift + col:shift + col + 1], in1=xT_hi[:, col, :],
                                                             op0=ALU.add, op1=ALU.subtract)
                ins.then_inc(xlo_ready, 1)

            for j in range(UPB):
                if j >= 2:
                    dve.wait_ge(xlo_ready, UPB * f + j - 1)
                if f == 0:
                    for k in range(2):
                        col = 2 * j + k
                        ins = nc.vector.tensor_scalar(norm_tmp[:, j % 2, k, :], xT_raw[:, col, :], scale_col[:, col:col + 1],
                                                      modT[:, shift + col:shift + col + 1], ALU.mult, ALU.add)
                else:
                    dve.wait_ge(staged, UPB * f + j + 1)
                    rows = psum[:, 4:5, 0:T].broadcast_to((P, 2, T))
                    ins = nc.vector.tensor_tensor(norm_tmp[:, j % 2], xT_raw[:, 2 * j:2 * j + 2, :], rows, ALU.mult)
                ins.then_inc(xm_ready, 1)
                if j:
                    lo(j - 1)
                    sub_units(first + j + 2)
                    if f != 1:
                        ada_peeled(f // 2)
            lo(UPB - 1)

        def prod(o, n):
            dve.wait_ge(unit_done, n.count())
            dve.wait_ge(silu_ready, o.count(plus=1))
            if o.n0:
                dve.wait_ge(act_turned, o.count())
            for s in range(HALF):
                ins = nc.vector.tensor_tensor(act_tok[:, s, :], silu_a[:, s, :], psum[:, 2 + s, :], ALU.mult)
            ins.then_inc(prod_ready, 1)

        def act_lo(o):
            dve.wait_ge(ahi_ready, o.count(plus=1))
            for j in range(2):
                ins = nc.vector.tensor_tensor(aT_lo[:, 2 * j:2 * j + 2, :],
                                              psum[:, 4 + j, :].rearrange("p (k t) -> p k t", k=2),
                                              aT_hi[:, 2 * j:2 * j + 2, :], ALU.subtract)
            ins.then_inc(alo_ready, 1)

        def y_add(o, q, n):
            bank = 6 if q % 2 == 0 else 4
            dve.wait_ge(unit_done, n.count())
            if o.n0 in (0, Y_MIX, Y_ADDS[1]) or o.per:
                dve.wait_ge(y_zero, 1 if o.n0 < Y_MIX else 2 if o.n0 < Y_ADDS[1] else 3)
            if o.n0:
                dve.wait_ge(y_added, o.count())
            for s in range(HALF):
                ins = nc.vector.tensor_tensor(y[:, s, q * NB:(q + 1) * NB], psum[:, bank + s, :],
                                              y[:, s, q * NB:(q + 1) * NB], ALU.add)
            ins.then_inc(y_added, 1)

        def ffn(f):
            n0 = ffn_base[f]
            o0 = f * FBLK
            for u in range(FIRST):
                sub_units(n0 + u + 1)
                ada_peeled(f)

            def hidden(n, o, adds, w0=0, ada=None):
                for u in range(BLOCK):
                    if n.per:
                        sub(n + u)
                        k = ada_unit_after("trip", w0 + u)
                        if ada and k is not None:
                            ada_add(At(ada.n0 * KT + k, KT, ada.trip), k)
                    else:
                        sub_units(n.n0 + u + 1)
                        ada_peeled(f)
                    if u == 2:
                        prod(o, n)
                    if u == 7:
                        act_lo(o)
                    if u in (12, 14, 16, 18):
                        q = (u - 12) // 2
                        y_add(adds + q, q, n + (UPB + 2 * q + 2))

            for e in range(2):
                hidden(At(n0 + FIRST + e * BLOCK), At(o0 + e), At(Y_ADDS[f] + e * QB))
                mod_out(At((ADA_FIRST, ADA_FFN2)[f] + e), 6)
            with dve.Fori(0, TRIPS) as trip:
                piece = At(ADA_FIRST + ADA_PEELED, 1, trip)
                for e in range(2):
                    hidden(At(n0 + PEELED + e * BLOCK, BODY, trip), At(o0 + 2 + e, 2, trip),
                           At(Y_ADDS[f] + (2 + e) * QB, 2 * QB, trip), e * BLOCK, piece if f == 0 else None)
                if f == 0:
                    mod_out(piece, 6)
            done[0] = n0 + FFN_UNITS - UPB
            n = At(done[0])
            sub_units(n.n0 + LAG)
            if f == 0:
                scale_out(1)
            prod(At(o0 + FBLK - 1), n)
            act_lo(At(o0 + FBLK - 1))
            finish(At(n.n0), Y_ADDS[f] + (FBLK - 1) * QB, 2 * f, 0.5)

        def finish(n, adds, k, factor):
            for q in range(QB):
                sub_units(n.n0 + min(2 * q + 4, UPB))
                y_add(At(adds + q), q, n + (2 * q + 2))
                if q == 0:
                    dve.wait_ge(gate_ready, k + 1)
                    if k == 1:
                        dve.wait_ge(h_loaded, 16)
                dve.wait_ge(y_added, adds + q + 1)
                cols = slice(q * NB, (q + 1) * NB)
                gate = psum[:, q:q + 1, :].broadcast_to((P, HALF, NB))
                nc.vector.scalar_tensor_tensor(out=y[:, :, cols], in0=gate, scalar=factor, in1=y[:, :, cols],
                                               op0=ALU.mult, op1=ALU.mult).then_inc(gated, 1)
                dve.wait_ge(gated, k * QB + q + 1)
                nc.vector.tensor_tensor(h[:, :, cols], h[:, :, cols], y[:, :, cols], ALU.add).then_inc(h_ready, 1)

        def pair(b):
            return 2 * (b % 2)

        def conv_tap(b, j):
            if j == 0:
                dve.wait_ge(pair_read[b % 2], b // 2 + 1)
                dve.wait_ge(pads, 1)
            channel = {"xs": 0, "b": 16, "c": 24}[kind[b]] + 4 * WBLOCKS[b][1]
            for k in range(4):
                if j:
                    dve.wait_ge(taps, 12 * b + 4 * (j - 1) + k + 1)
                col = 32 * j + channel + k
                nc.vector.scalar_tensor_tensor(out=conv[:, k, :], in0=padded[:, b % 2, k, j:j + T],
                                               scalar=convT[:, col:col + 1], in1=conv[:, k, :],
                                               op0=ALU.mult, op1=ALU.add).then_inc(taps, 1)

        steps = [0]

        def dt_do(ins):
            ins.then_inc(dt_step, 1)
            steps[0] += 1
            dve.wait_ge(dt_step, steps[0])

        def dt_first():
            dve.wait_ge(front_turned, 1)
            dt_do(nc.vector.tensor_tensor(sp_v[:], psum[:, 4, 0:2 * FRONT_COLS].rearrange("p (s n) -> p s n", s=2)[:, :, 0:SSD_H],
                                          dt_bias[:].rearrange("p (o n) -> p o n", o=1).broadcast_to((P, HALF, SSD_H)), ALU.add))
            dt_do(nc.vector.scalar_tensor_tensor(out=sp_e[:], in0=sp_v[:], scalar=-1.0, in1=sp_v[:], op0=ALU.mult, op1=ALU.max))

        def dt_rest():
            dve.wait_ge(dt_exp, 1)
            dt_do(nc.vector.tensor_scalar(sp_s[:], sp_e[:], 2.0, None, ALU.add))
            dt_do(nc.vector.reciprocal(sp_s[:], sp_s[:]))
            dt_do(nc.vector.tensor_tensor(sp_s[:], sp_s[:], sp_e[:], ALU.mult))
            dt_do(nc.vector.tensor_tensor(sp_e[:], sp_s[:], sp_s[:], ALU.mult))
            dt_do(nc.vector.tensor_scalar(sp_p[:], sp_e[:], 1.0 / 17.0, None, ALU.mult))
            for k in range(15, 1, -2):
                dt_do(nc.vector.scalar_tensor_tensor(out=sp_p[:], in0=sp_p[:], scalar=1.0 / k, in1=sp_e[:],
                                                     op0=ALU.add, op1=ALU.mult))
            dt_do(nc.vector.scalar_tensor_tensor(out=sp_p[:], in0=sp_p[:], scalar=1.0, in1=sp_s[:],
                                                 op0=ALU.add, op1=ALU.mult))
            dt_do(nc.vector.tensor_scalar(sp_v[:], sp_v[:], 0.0, None, ALU.max))
            dt_do(nc.vector.scalar_tensor_tensor(out=dt[:], in0=sp_p[:], scalar=2.0, in1=sp_v[:],
                                                 op0=ALU.mult, op1=ALU.add))
            dve.wait_ge(a_exp_ready, 1)
            nc.vector.scalar_tensor_tensor(out=dta[:], in0=dt[:], scalar=-1.0,
                                           in1=a_exp[:].rearrange("p (o n) -> p o n", o=1).broadcast_to((P, HALF, SSD_H)),
                                           op0=ALU.mult, op1=ALU.mult).then_inc(dta_ready, 1)

        def cum_out():
            dve.wait_ge(cum_ready, 1)
            dt_do(nc.vector.tensor_scalar(acum[:, 0:2, :], psum[:, 4, 0:64].rearrange("p (s n) -> p s n", s=2),
                                          -1.0, None, ALU.mult))
            nc.vector.tensor_tensor(acum[:, 2, :], psum[:, 4, 64:96], acum[:, 0, :], ALU.add).then_inc(acum_ready, 1)

        def ssd_segments(g):
            dve.wait_ge(cb_ready, g + 1)
            dve.wait_ge(acum_ready, 1)
            if g:
                dve.wait_ge(y_raw, g)
                dve.wait_ge(masked_ready, g)
            for j, bank, col in ((0, 5, 0), (1, 6, 2), (2, 6, 1)):
                for k in range(4):
                    nc.vector.tensor_scalar(decay[:, j, k, :], psum[:, bank, k * P:(k + 1) * P],
                                            acum[:, col, 4 * g + k:4 * g + k + 1], 0.0, ALU.add, ALU.min)
            nc.vector.tensor_tensor(cb[:, 0, :], psum[:, 4, 0:P], upper[:], ALU.mult)
            nc.vector.tensor_copy(cb[:, 1, :], psum[:, 4, P:2 * P])
            nc.vector.tensor_tensor(cb[:, 2, :], psum[:, 4, 2 * P:3 * P], upper[:], ALU.mult).then_inc(seg_ready, 1)

        heads4 = lambda t: t.rearrange("p s (k d) -> p s k d", k=4)

        def per_head(t, g):
            return t[:, :, 4 * g:4 * g + 4].rearrange("p s (k o) -> p s k o", o=1).broadcast_to((P, HALF, 4, 64))

        def ssd_mask(g):
            dve.wait_ge(decay_ready, g + 1)
            dve.wait_ge(seg_ready, g + 1)
            dve.wait_ge(xs_ready, g // 2 + 1)
            nc.vector.tensor_tensor(xdt[:], heads4(xs[:, g]), per_head(dt, g), ALU.mult)
            for j in range(3):
                ins = nc.vector.tensor_tensor(decay[:, j], decay[:, j], cb[:, j:j + 1, :].broadcast_to((P, 4, P)), ALU.mult)
            ins.then_inc(masked_ready, 1)

        def ssd_gate(g):
            zb = at_block["z"] + g // 2
            dve.wait_ge(pair_read[zb % 2], zb // 2 + 1)
            if g:
                dve.wait_ge(y_normed, g)
                dve.wait_ge(y_turned, g)
            skips = skip[:, 4 * g:4 * g + 4].rearrange("p (o k q) -> p o k q", o=1, q=1).broadcast_to((P, HALF, 4, 64))
            nc.vector.tensor_tensor(heads4(yg[:]), heads4(xs[:, g]), skips, ALU.mult).then_inc(y_step, 1)
            dve.wait_ge(y_raw, g + 1)
            dve.wait_ge(y_step, 2 * g + 1)
            nc.vector.tensor_tensor(yg2[:], psum[:, 7, :].rearrange("p (s n) -> p s n", s=2), yg[:], ALU.add).then_inc(y_step, 1)
            dve.wait_ge(y_step, 2 * g + 2)
            nc.vector.tensor_tensor(yg[:], yg2[:], zs[:, g], ALU.mult).then_inc(y_gated, 1)

        def ssd_norm_out(g):
            dve.wait_ge(y_rstd_ready, g + 1)
            for half in range(HALF):
                ins = nc.vector.tensor_scalar(yg2[:, half, :], yg[:, half, :], y_rstd[:, half:half + 1], None, ALU.mult)
            ins.then_inc(y_normed, 1)

        def y_lo_out(g):
            dve.wait_ge(y_hi, g + 1)
            for k in range(2):
                ins = nc.vector.scalar_tensor_tensor(out=yT_lo[:, 2 * g + k, :], in0=psum[:, 4, k * T:(k + 1) * T],
                                                     scalar=vecT[:, 64 + 2 * g + k:65 + 2 * g + k],
                                                     in1=yT_hi[:, 2 * g + k, :], op0=ALU.mult, op1=ALU.subtract)
            ins.then_inc(y_lo, 1)

        def head_sum(i):
            dve.wait_ge(sq_ready, i + 1)
            nc.vector.tensor_reduce(h_sum[:], sq[:].rearrange("p s (k d) -> p (s k) d", d=HD), AX.X, ALU.add).then_inc(head_sums, 1)

        def head_norm(i, b):
            dve.wait_ge(head_rstd, i + 1)
            if i:
                dve.wait_ge(head_turned, 2 * i - 1)
            for half in range(HALF):
                r = h_rstd[:, 4 * half:4 * half + 4].rearrange("p (k o) -> p k o", o=1).broadcast_to((P, 4, HD))
                ins = nc.vector.tensor_tensor(qn[:, half, :].rearrange("p (k d) -> p k d", k=4),
                                              psum[:, pair(b) + half, :].rearrange("p (k d) -> p k d", k=4), r, ALU.mult)
            ins.then_inc(pair_read[b % 2], 1)

        def index_add(j):
            dve.wait_ge(rel_ready, j + 1)
            for e in range(2):
                for half in range(HALF):
                    head = 2 * j + e
                    i = 2 * head + half
                    if i < 2:
                        ins = nc.vector.tensor_scalar(score[:, half, :], rel[:, e, half, :], wi[:, half, head:head + 1], None, ALU.mult)
                    else:
                        dve.wait_ge(score_step, i - 1)
                        ins = nc.vector.scalar_tensor_tensor(out=score[:, half, :], in0=rel[:, e, half, :],
                                                             scalar=wi[:, half, head:head + 1], in1=score[:, half, :],
                                                             op0=ALU.mult, op1=ALU.add)
                    ins.then_inc(score_step, 1)

        tops = [0]

        def top_do(ins):
            ins.then_inc(top_step, 1)
            tops[0] += 1

        def top_wait(back=0):
            dve.wait_ge(top_step, tops[0] - back)

        def admit():
            dve.wait_ge(score_step, 4 * 8)
            dve.wait_ge(pos_ready, 3)
            for half in range(HALF):
                top_do(nc.vector.tensor_scalar(banned[:, half, :], key_chunk[:], query_chunk[:, half:half + 1], NEG,
                                               ALU.is_gt, ALU.mult))
            for half in range(HALF):
                top_do(nc.vector.tensor_scalar(dist[:, half, :], key_pos[:], query_pos[:, half:half + 1], None,
                                               ALU.subtract))
            top_wait()
            top_do(nc.vector.scalar_tensor_tensor(out=dist[:], in0=dist[:], scalar=-1.0, in1=dist[:],
                                                  op0=ALU.mult, op1=ALU.max))
            for half in range(HALF):
                top_do(nc.vector.tensor_tensor(score[:, half, :], score[:, half, :], banned[:, half, :], ALU.add))

        def top_round():
            for half in range(HALF):
                top_wait(1)
                top_do(nc.vector.max(top8[:, half, :], score[:, half, :]))
            for half in range(HALF):
                top_wait(1)
                top_do(nc.vector.match_replace(score[:, half, :], top8[:, half, :], score[:, half, :], TAKEN))

        def top_out():
            top_wait()
            top_do(nc.vector.tensor_scalar(score[:], score[:], TAKEN, MASKED, ALU.not_equal, ALU.mult))
            top_do(nc.vector.scalar_tensor_tensor(out=dist[:], in0=banned[:], scalar=-1.0, in1=dist[:], op0=ALU.mult, op1=ALU.add))
            top_wait()
            nc.vector.tensor_tensor(dist[:], dist[:], score[:], ALU.add).then_inc(dist_ready, 1)

        def logits_out(a):
            dve.wait_ge(logits_done, a + 1)
            if a == 0:
                dve.wait_ge(dist_ready, 1)
            if a >= 2:
                dve.wait_ge(probs_turned, a - 1)
            slope = 2.0 ** (-8.0 * (a + 1) / HEADS)
            nc.vector.scalar_tensor_tensor(out=probs[:, a % 2], in0=dist[:], scalar=-slope,
                                           in1=psum[:, 5, :].rearrange("p (s t) -> p s t", s=2),
                                           op0=ALU.mult, op1=ALU.add).then_inc(logit_step, 1)
            dve.wait_ge(logit_step, a + 1)
            nc.vector.tensor_reduce(row_max[:, a % 2, :], probs[:, a % 2], AX.X, ALU.max, negate=True).then_inc(logits_ready, 1)

        def probs_norm(a):
            dve.wait_ge(exp_done, a + 1)
            nc.vector.reciprocal(row_inv[:, a % 2, :], row_sum[:, a % 2, :]).then_inc(inv_ready, 1)
            dve.wait_ge(inv_ready, a + 1)
            nc.vector.tensor_tensor(probs[:, a % 2], probs[:, a % 2],
                                    row_inv[:, a % 2, :].rearrange("p (s o) -> p s o", o=1).broadcast_to((P, HALF, T)),
                                    ALU.mult).then_inc(probs_ready, 1)

        def o_lo_out(a):
            dve.wait_ge(o_hi, a + 1)
            nc.vector.tensor_tensor(oT_lo[:, a, :], psum[:, 4, 0:T], oT_hi[:, a, :], ALU.subtract).then_inc(o_lo, 1)

        def merge_ssd(n, b):
            dve.wait_ge(unit_done, n.count())
            dve.wait_ge(pair_read[0], (b + NW // 2 + 1).count() if not b.per else At(NW // 2 + 1 + 2 * b.n0, 2, b.trip).count())
            for half in range(HALF):
                ins = nc.vector.tensor_tensor(sg0[:, half, :], sg0[:, half, :], psum[:, half, :], ALU.mult)
            ins.then_inc(pair_read[0], 1)

        def merge_att(n, b):
            dve.wait_ge(unit_done, n.count())
            dve.wait_ge(pair_read[1], (b + NW // 2 + 1).count() if not b.per else At(NW // 2 + 1 + 2 * b.n0, 2, b.trip).count())
            for half in range(HALF):
                ins = nc.vector.tensor_tensor(sg1[:, half, :], sg1[:, half, :], psum[:, 2 + half, :], ALU.mult)
            ins.then_inc(pair_read[1], 1)
            dve.wait_ge(pair_read[1], At(NW // 2 + 2 + 2 * b.n0, 2 if b.per else 0, b.trip).count())
            dve.wait_ge(pair_read[0], At(NW // 2 + 2 + 2 * b.n0, 2 if b.per else 0, b.trip).count())
            nc.vector.tensor_tensor(sg0[:], sg0[:], sg1[:], ALU.add).then_inc(merged, 1)

        def merged_lo(b):
            dve.wait_ge(m_hi, b.count(plus=1))
            for j in range(2):
                ins = nc.vector.tensor_tensor(mT_lo[:, 2 * j:2 * j + 2, :], psum[:, 4 + j, :].rearrange("p (k t) -> p k t", k=2),
                                              mT_hi[:, 2 * j:2 * j + 2, :], ALU.subtract)
            ins.then_inc(m_lo, 1)

        def mixer():
            mix_ada = ADA_MIX * KT
            for n in range(MIX, M1):
                sub_units(n + 1)
                if n not in FRONT_UNITS and n < start[at_block["qi"]] and (n - (MIX if n < FRONT else FRONT_END)) % 2:
                    ada_add(At(mix_ada), mix_ada % KT)
                    mix_ada += 1
                for i in range(ADA_MIXED):
                    if n == start[4 * (i + 1)] + 4:
                        mod_out(At(ADA_MIX + i), 7)
                for b in range(NW):
                    if kind[b] in ("b", "c", "xs") and n in (end[b] + 3, end[b] + 4, end[b] + 5):
                        conv_tap(b, n - end[b] - 3)
                    i = 0 if kind[b] == "k" else 1 + WBLOCKS[b][1]
                    if kind[b] in ("k", "q") and n == end[b] + 2:
                        head_sum(i)
                    if kind[b] in ("k", "q") and n == end[b] + 4:
                        head_norm(i, b)
                if n == FRONT_END + 5:
                    dt_first()
                if n == FRONT_END + 7:
                    dt_rest()
                if n == FRONT_END + 2 * UPB + 2:
                    cum_out()
                for g in range(GROUPS):
                    s = ssd_start[g]
                    if n == s + 2:
                        ssd_segments(g)
                    if n == s + 4:
                        ssd_mask(g)
                    if n == s + 7:
                        ssd_gate(g)
                    if n == s + 9:
                        ssd_norm_out(g)
                    if n == s + 12:
                        y_lo_out(g)
                for j in range(8):
                    if n == index_slot[j] + 3:
                        index_add(j)
                s = start[at_block["q"]]
                if n == s + 2:
                    admit()
                if s + 3 <= n < s + 3 + TOPK // 8:
                    top_round()
                if n == s + 3 + TOPK // 8:
                    top_out()
                for a in range(HEADS):
                    if n == att_slot[a] + 2:
                        logits_out(a)
                    if n == att_slot[a] + 4:
                        probs_norm(a)
                    if n == att_slot[a] + 9:
                        o_lo_out(a)
                if n == M0 + 3 * UPB + 2:
                    merge_ssd(At(M0 + 3 * UPB), At(0))
                if n == M1 - 1:
                    dve.wait_ge(o_done, HEADS)
                    nc.vector.memset(y[:], 0.0).then_inc(y_zero, 1)
            with dve.Fori(0, QB - 1) as trip:
                m = At(M1, MBODY, trip)
                for u in range(MBODY):
                    sub(m + u)
                    k = ada_unit_after("merge", u)
                    if k is not None:
                        ada_add(At(ADA_MERGE * KT + k, KT, trip), k)
                    if u == MBODY - 2:
                        mod_out(At(ADA_MERGE, 1, trip), 7)
                    if u == 2:
                        merge_att(m, At(0, 1, trip))
                    if u == 7:
                        merged_lo(At(0, 1, trip))
                    if u in (20, 22, 24, 26):
                        q = (u - 20) // 2
                        y_add(At(Y_MIX + q, QB, trip), q, m + (2 * UPB + 2 * q + 2))
                    if u == 4 * UPB + 2:
                        merge_ssd(m + 4 * UPB, At(1, 1, trip))
            done[0] = MEND
            sub_units(MEND + LAG)
            merge_att(At(MEND), At(QB - 1))
            merged_lo(At(QB - 1))
            scale_out(2)
            finish(At(MEND), Y_MIX + (QB - 1) * QB, 1, 1.0)

        norm(0)
        ffn(0)
        norm(1)
        mixer()
        norm(2)
        ffn(1)

    @block.tensor
    def _(pe):
        def turn(dst, src, rows_=P):
            return nc.tensor.transpose(dst, src, ident[0:rows_, 0:rows_])

        def unit(n, hi, lo, kt, bank, first, last):
            pe.wait_ge(split_ready, n.count(plus=1))
            s = n.slot(SPLIT)
            for half in range(HALF):
                toks = slice(half * P, (half + 1) * P)
                for k in range(2):
                    whi, wlo = w_hi[:, s, k * NB:(k + 1) * NB], w_lo[:, s, k * NB:(k + 1) * NB]
                    o = psum[:, bank + half, :]
                    a, b = first and k == 0, last and k == 1
                    nc.tensor.matmul(o, hi[:, kt + k, toks], whi, start=a, stop=False)
                    nc.tensor.matmul(o, hi[:, kt + k, toks], wlo, start=False, stop=False)
                    ins = nc.tensor.matmul(o, lo[:, kt + k, toks], whi, start=False, stop=b)
            ins.then_inc(unit_done, 1)

        def sum_ada(bank, acc=ada_acc[0]):
            for j in range(8):
                ins = nc.tensor.matmul(psum[:, bank, j:j + 1], acc[:, j * P:(j + 1) * P], ones[:, 0:1],
                                       start=True, stop=True)
            ins.then_inc(ada_summed, 1)

        def turn_act(o):
            pe.wait_ge(prod_ready, o.count(plus=1))
            for k in range(4):
                for half in range(HALF):
                    ins = turn(psum[:, 4 + k // 2, (k % 2) * T + half * P:(k % 2) * T + (half + 1) * P],
                               act_tok[:, half, k * P:(k + 1) * P])
            ins.then_inc(act_turned, 1)

        pe.wait_ge(consts, 6)
        pe.wait_ge(c_in, 16)
        turn(psum[:, 1, 0:KT], c_row[0:KT, :], KT).then_inc(c_turned, 1)
        pe.wait_ge(rows_in, 16 * 11)
        turn(psum[:, 0, 0:114], vecs[0:114, :], 114)
        turn(psum[:, 0, 128:256], convs[:])
        turn(psum[:, 0, 256:384], badas[:, 0, :])
        turn(psum[:, 0, 384:400], badas[0:16, 1, :], 16).then_inc(rows_turned, 1)

        def turn_x(f, j, src):
            bank = turn_bank(f, j)
            for k in range(2):
                for half in range(HALF):
                    ins = turn(psum[:, bank, k * T + half * P:k * T + (half + 1) * P],
                               src[:, half, (2 * j + k) * P:(2 * j + k + 1) * P])
            ins.then_inc(xn_turned, 1)

        for e in range(ADA_FIRST):
            pe.wait_ge(ada_used, (e + 1) * KT)
            pe.wait_ge(mod_ready, e) if e else pe.wait_ge(cols_ready, 1)
            sum_ada(0, ada_acc[e % 2])
            if e == 1:
                pe.wait_ge(xn_ready, 2)
                for j in range(UPB):
                    if j >= 2:
                        pe.wait_ge(staged, j - 1)
                    turn_x(0, j, y)

        def turn_h(f, j):
            pe.wait_ge(h_ready, (f - 1) * QB + j // 2 + 1)
            if j:
                pe.wait_ge(staged, UPB * f + (1 if j == 1 else j - 1))
            turn_x(f, j, h)

        def turn_tail(f, u):
            if u >= 4:
                turn_h(f, u - 4)
            if u == UPB:
                for j in range(5, UPB):
                    turn_h(f, j)
                pe.wait_ge(rstd_ready, f + 1)
                for half in range(HALF):
                    ins = nc.tensor.matmul(psum[:, 4, half * P:(half + 1) * P], rstd[:, half:half + 1].broadcast_to((P, P)),
                                           ident[:], start=True, stop=True)
                ins.then_inc(row_ready, 1)

        def ffn(f):
            n0 = ffn_base[f]
            o0 = f * FBLK
            for u in range(UPB):
                pe.wait_ge(xlo_ready, UPB * 2 * f + max(u + 1, 2))
                unit(At(n0 + u), xT_hi, xT_lo, 2 * u, 0, u == 0, u == UPB - 1)
            for u in range(UPB):
                unit(At(n0 + UPB + u), xT_hi, xT_lo, 2 * u, 2, u == 0, u == UPB - 1)

            def hidden(n, o, adds, mods=None, ada=None):
                pe.wait_ge(silu_ready, o.count(plus=1))
                for u in range(UPB):
                    if u == 5:
                        if adds.n0:
                            pe.wait_ge(y_added, adds.count())
                        turn_act(o)
                    unit(n + u, xT_hi, xT_lo, 2 * u, 0, u == 0, u == UPB - 1)
                for q in range(QB):
                    bank = 6 if q % 2 == 0 else 4
                    if q == 0:
                        pe.wait_ge(alo_ready, o.count(plus=1))
                        pe.wait_ge(mod_ready, mods.count())
                    if q >= 2:
                        pe.wait_ge(y_added, (adds + (q - 1)).count())
                    for k in range(2):
                        unit(n + (UPB + 2 * q + k), aT_hi, aT_lo, 2 * k, bank, k == 0, k == 1)
                for u in range(UPB):
                    if 2 * UPB + u == ADA_SUM_AT:
                        pe.wait_ge(y_added, (adds + QB).count())
                        if ada:
                            pe.wait_ge(ada_used, At((ada.n0 + 1) * KT, ada.per * KT, ada.trip).count())
                            sum_ada(6, ada_acc[0 if ada.per else ada.n0 % 2])
                    unit(n + (2 * UPB + u), xT_hi, xT_lo, 2 * u, 2, u == 0, u == UPB - 1)

            ada0 = (ADA_FIRST, ADA_FFN2)[f]
            for e in range(2):
                hidden(At(n0 + FIRST + e * BLOCK), At(o0 + e), At(Y_ADDS[f] + e * QB), At(ada0 + e), At(ada0 + e))
            with pe.Fori(0, TRIPS) as trip:
                piece = At(ada0 + ADA_PEELED, 1 if f == 0 else 0, trip)
                for e in range(2):
                    hidden(At(n0 + PEELED + e * BLOCK, BODY, trip), At(o0 + 2 + e, 2, trip),
                           At(Y_ADDS[f] + (2 + e) * QB, 2 * QB, trip), piece, piece if f == 0 and e == 1 else None)
            n = At(n0 + FFN_UNITS - UPB)
            turn_act(At(o0 + FBLK - 1))
            spread_gate((2, 8)[f])
            pe.wait_ge(alo_ready, o0 + FBLK)
            if f == 0:
                pe.wait_ge(mod_ready, ADA_MIX)
            for q in range(QB):
                if q >= 2:
                    pe.wait_ge(y_added, Y_ADDS[f] + (FBLK - 1) * QB + q - 1)
                bank = 6 if q % 2 == 0 else 4
                for k in range(2):
                    if f == 0:
                        turn_tail(1, 2 * q + k)
                    unit(n + (2 * q + k), aT_hi, aT_lo, 2 * k, bank, k == 0, k == 1)
            if f == 0:
                turn_tail(1, UPB)

        def fm_unit(n, kt, bank, first, last):
            pe.wait_ge(split_ready, n + 1)
            s = n % SPLIT
            for j in range(4):
                o = psum[:, bank + j // 2, (j % 2) * T:(j % 2 + 1) * T]
                for k in range(2):
                    cols = slice(k * NB + j * P, k * NB + (j + 1) * P)
                    a, b = first and k == 0 and j % 2 == 0, last and k == 1
                    nc.tensor.matmul(o, w_hi[:, s, cols], xT_hi[:, kt + k, :], start=a, stop=False, skip_group_check=True)
                    nc.tensor.matmul(o, w_hi[:, s, cols], xT_lo[:, kt + k, :], start=False, stop=False, skip_group_check=True)
                    ins = nc.tensor.matmul(o, w_lo[:, s, cols], xT_hi[:, kt + k, :], start=False, stop=b, skip_group_check=True)
            ins.then_inc(unit_done, 1)

        def front_unit(n):
            pe.wait_ge(split_ready, n + 1)
            s = n % SPLIT
            o = psum[0:FRONT_COLS, 5, 0:T]
            for kk in range(FRONT_KT):
                k = FRONT_KT * (n - FRONT) + kk
                w = slice(kk * FRONT_COLS, (kk + 1) * FRONT_COLS)
                nc.tensor.matmul(o, w_hi[:, s, w], xT_hi[:, k, :], start=k == 0, stop=False)
                nc.tensor.matmul(o, w_hi[:, s, w], xT_lo[:, k, :], start=False, stop=False)
                ins = nc.tensor.matmul(o, w_lo[:, s, w], xT_hi[:, k, :], start=False, stop=k == KT - 1)
            ins.then_inc(unit_done, 1)

        def spread_gate(chunk):
            for k in range(KT):
                col = chunk * KT + k
                ins = nc.tensor.matmul(psum[:, k // 4, (k % 4) * P:(k % 4 + 1) * P],
                                       modT[:, col:col + 1].broadcast_to((P, P)), ident[:], start=True, stop=True)
            ins.then_inc(gate_ready, 1)

        def plain(o, a, b, first=True, last=True):
            return nc.tensor.matmul(o, a, b, start=first, stop=last)

        def turn_xs(b):
            pe.wait_ge(conv_out, b + 1)
            i = WBLOCKS[b][1]
            if i:
                pe.wait_ge(xs_ready, i)
            for half in range(HALF):
                for k in range(4):
                    ins = turn(psum[:, 4 + half, k * P:(k + 1) * P], conv[:, k, half * P:(half + 1) * P])
            ins.then_inc(xs_turned, 1)

        def cumulate():
            pe.wait_ge(dta_ready, 1)
            pe.wait_ge(front_read, 1)
            for half in range(HALF):
                plain(psum[:, 4, half * SSD_H:(half + 1) * SSD_H], upper[:], dta[:, half, :])
            plain(psum[:, 4, 64:96], ones[:], dta[:, 0, :]).then_inc(cum_ready, 1)

        def ssd_products(g):
            if g == 0:
                pe.wait_ge(xs_ready, 4)
            if g:
                pe.wait_ge(seg_ready, g)
            if g >= 2:
                pe.wait_ge(y_lo, g - 1)
            if g == 6:
                pe.wait_ge(rel_ready, 4)
            if g == 7:
                pe.wait_ge(head_ready, 1)
            plain(psum[:, 4, 0:T], bT[:, g, 0:P], cT[:, g, :])
            plain(psum[:, 4, T:T + P], bT[:, g, P:T], cT[:, g, P:T])
            for half in range(HALF):
                for k in range(4):
                    ins = plain(psum[:, 5 + half, k * P:(k + 1) * P],
                                dta[:, half, 4 * g + k:4 * g + k + 1].broadcast_to((P, P)), upper[:])
            ins.then_inc(cb_ready, 1)

        def ssd_y(g):
            pe.wait_ge(masked_ready, g + 1)
            if g:
                pe.wait_ge(y_gated, g)
            if g == 3:
                pe.wait_ge(mod_ready, ADA_MERGE)
            for k in range(4):
                plain(psum[:, 7, k * 64:(k + 1) * 64], decay[:, 0, k, :], xdt[:, 0, k, :])
                o = psum[:, 7, T + k * 64:T + (k + 1) * 64]
                plain(o, decay[:, 1, k, :], xdt[:, 0, k, :], True, False)
                ins = plain(o, decay[:, 2, k, :], xdt[:, 1, k, :], False, True)
            ins.then_inc(y_raw, 1)

        def turn_y(g):
            pe.wait_ge(y_normed, g + 1)
            pe.wait_ge(seg_ready, min(g + 2, GROUPS))
            for k in range(2):
                for half in range(HALF):
                    ins = turn(psum[:, 4, k * T + half * P:k * T + (half + 1) * P], yg2[:, half, k * P:(k + 1) * P])
            ins.then_inc(y_turned, 1)

        def index(j):
            if j == 0:
                qb = at_block["qi"] + 1
                pe.wait_ge(pair_read[(qb - 1) % 2], (qb - 1) // 2 + 1)
                pe.wait_ge(pair_read[qb % 2], qb // 2 + 1)
                pe.wait_ge(kiT_ready, 1)
            else:
                pe.wait_ge(rel_ready, j)
            pe.wait_ge(seg_ready, 6 if j < 4 else 7)
            for half in range(HALF):
                for e in range(2):
                    rows = slice(64 * e, 64 * e + 64)
                    ins = plain(psum[:, 5 + e, half * T:(half + 1) * T], qiT[rows, j, half * P:(half + 1) * P], kiT[rows, :])
            ins.then_inc(index_done, 1)

        def turn_heads(heads, bank):
            for i, k in enumerate(heads):
                for half in range(HALF):
                    ins = turn(psum[:, bank, i * T + half * P:i * T + (half + 1) * P], qn[:, half, k * HD:(k + 1) * HD])
            return ins

        def turn_k(b):
            pe.wait_ge(pair_read[b % 2], b // 2 + 1)
            pe.wait_ge(rel_ready, 8)
            turn_heads((0, 1), 5)
            turn_heads((2, 3), 6).then_inc(head_turned, 1)

        def turn_q(b, i, j):
            pe.wait_ge(pair_read[b % 2], b // 2 + 1)
            pe.wait_ge(y_gated, GROUPS)
            pe.wait_ge(head_ready, 1 + 2 * i + j)
            turn_heads((2 * j, 2 * j + 1), 7).then_inc(head_turned, 1)

        def logits(a):
            g, m = divmod(a, 4)
            pe.wait_ge(head_ready, 1 + 2 * g + m // 2 + 1)
            if a:
                pe.wait_ge(logits_ready, a)
            for half in range(HALF):
                ins = plain(psum[:, 5, half * T:(half + 1) * T], qT[:, m, half * P:(half + 1) * P], kT[:, g, :])
            ins.then_inc(logits_done, 1)

        def turn_probs(a):
            pe.wait_ge(probs_ready, a + 1)
            if a:
                pe.wait_ge(pT_ready, a)
            for k in range(2):
                for half in range(HALF):
                    ins = turn(psum[:, 6, k * T + half * P:k * T + (half + 1) * P], probs[:, a % 2, half, k * P:(k + 1) * P])
            ins.then_inc(probs_turned, 1)

        def attend(a):
            g = a // 4
            pe.wait_ge(pT_ready, a + 1)
            pe.wait_ge(o_lo, a) if a else pe.wait_ge(y_lo, GROUPS)
            if a == 0:
                vb = at_block["v"]
                pe.wait_ge(pair_read[vb % 2], vb // 2 + 1)
            for k in range(2):
                ins = plain(psum[:, 4, 0:T], vt[:, k, g * HD:(g + 1) * HD], pT[:, a % 2, k, :], k == 0, k == 1)
            ins.then_inc(o_done, 1)

        def turn_merged(b, adds=None):
            pe.wait_ge(merged, b.count(plus=1))
            if adds is None:
                pe.wait_ge(o_lo, HEADS)
            else:
                pe.wait_ge(y_added, adds.count())
            for k in range(4):
                for half in range(HALF):
                    ins = turn(psum[:, 4 + k // 2, (k % 2) * T + half * P:(k % 2) * T + (half + 1) * P],
                               sg0[:, half, k * P:(k + 1) * P])
            ins.then_inc(merged_turned, 1)

        def out_quarter(n, q, adds, tail=False):
            if q >= 2:
                pe.wait_ge(y_added, (adds + (q - 1)).count())
            bank = 6 if q % 2 == 0 else 4
            for k in range(2):
                if tail:
                    turn_tail(2, 2 * q + k)
                unit(n + (2 * q + k), mT_hi, mT_lo, 2 * k, bank, k == 0, k == 1)

        def free_pair(which, count):
            pe.wait_ge(pair_read[which], count.count())

        def mixer():
            for n in range(MIX, M0):
                for i in range(ADA_MIXED):
                    if n == start[4 * (i + 1)] + 2:
                        pe.wait_ge(ada_used, (ADA_MIX + i + 1) * KT)
                        if i == 2:
                            pe.wait_ge(y_gated, 3)
                        sum_ada(7)
                for b in range(NW):
                    if kind[b] == "xs" and n == end[b] + 7:
                        turn_xs(b)
                    if kind[b] == "k" and n == end[b] + 7:
                        turn_k(b)
                    if kind[b] == "q" and n in (end[b] + 5, end[b] + 7):
                        turn_q(b, WBLOCKS[b][1], (n - end[b] - 5) // 2)
                if n == FRONT_END + 4:
                    pe.wait_ge(front_copied, 1)
                    for half in range(HALF):
                        ins = turn(psum[:, 4, half * FRONT_COLS:(half + 1) * FRONT_COLS],
                                   front_fm[0:FRONT_COLS, half * P:(half + 1) * P], FRONT_COLS)
                    ins.then_inc(front_turned, 1)
                if n == FRONT_END + 9:
                    pe.wait_ge(front_read, 1)
                    for half in range(HALF):
                        ins = turn(psum[:, 5, half * P:(half + 1) * P], ki_tok[:, half].rearrange("p e n -> p (e n)"))
                    ins.then_inc(ki_turned, 1)
                if n == FRONT_END + 2 * UPB:
                    cumulate()
                side(n)
                if n in FRONT_UNITS:
                    front_unit(n)
                    continue
                b = max(i for i in range(NW) if start[i] <= n)
                u = n - start[b]
                if b >= 2 and u == 0:
                    pe.wait_ge(pair_read[b % 2], b // 2)
                if b == 0:
                    pe.wait_ge(xlo_ready, UPB + max(u + 1, 2))
                if kind[b] in ("b", "c", "xs", "qi"):
                    fm_unit(n, 2 * u, 2 * (b % 2), u == 0, u == UPB - 1)
                else:
                    unit(At(n), xT_hi, xT_lo, 2 * u, 2 * (b % 2), u == 0, u == UPB - 1)
            for n in range(M0, M1):
                b = NW - 1
                if n in (end[b] + 5, end[b] + 7):
                    turn_q(b, 3, (n - end[b] - 5) // 2)
                side(n)
                part, u = divmod(n - M0, UPB)
                merge_unit(At(n), part, u, At(NW // 2 + part // 2))
            with pe.Fori(0, QB - 1) as trip:
                m = At(M1, MBODY, trip)
                for part in range(5):
                    for u in range(UPB):
                        if part * UPB + u == MBODY - 4:
                            pe.wait_ge(ada_used, At((ADA_MERGE + 1) * KT, KT, trip).count())
                            pe.wait_ge(y_added, At(Y_MIX + QB, QB, trip).count())
                            sum_ada(7)
                        if part == 0 and u == 5:
                            turn_merged(At(0, 1, trip), At(Y_MIX, QB, trip))
                        if part == 2:
                            if u == 0:
                                pe.wait_ge(mod_ready, At(ADA_MERGE, 1, trip).count())
                                pe.wait_ge(m_lo, At(1, 1, trip).count())
                            if u % 2 == 0:
                                out_quarter(m + 2 * UPB, u // 2, At(Y_MIX, QB, trip))
                        else:
                            p = part if part < 2 else part - 1
                            merge_unit(m + (part * UPB + u), p, u, At(NW // 2 + 2 + p // 2, 2, trip))
            turn_merged(At(QB - 1), At(Y_MIX + (QB - 1) * QB))
            free_pair(0, At(NW // 2 + 2 * QB))
            free_pair(1, At(NW // 2 + 2 * QB))
            pe.wait_ge(mod_ready, ADA_FFN2)
            spread_gate(5)
            pe.wait_ge(m_lo, QB)
            for q in range(QB):
                out_quarter(At(MEND), q, At(Y_MIX + (QB - 1) * QB), tail=True)
            turn_tail(2, UPB)

        def merge_unit(n, part, u, reads):
            if u == 0:
                free_pair(part % 2, reads)
                if part == 2:
                    pe.wait_ge(y_lo, GROUPS)
                if part == 3:
                    pe.wait_ge(o_lo, HEADS)
            hi, lo = ((xT_hi, xT_lo), (xT_hi, xT_lo), (yT_hi, yT_lo), (oT_hi, oT_lo))[part]
            unit(n, hi, lo, 2 * u, 2 * (part % 2), u == 0, u == UPB - 1)

        def side(n):
            for g in range(GROUPS):
                s = ssd_start[g]
                if n == s:
                    ssd_products(g)
                if n == s + 5:
                    ssd_y(g)
                if n == s + 10:
                    turn_y(g)
            for j in range(8):
                if n == index_slot[j]:
                    index(j)
            for a in range(HEADS):
                if n == att_slot[a]:
                    logits(a)
                if n == att_slot[a] + 4:
                    turn_probs(a)
                if n == att_slot[a] + 7:
                    attend(a)

        ffn(0)
        mixer()
        ffn(1)

    ctx.close()


_INS = ['x', 'c', 'positions', 'w_ada', 'b_ada', 'norm_ffn1', 'ffn1_w1', 'ffn1_w3', 'ffn1_w2', 'norm_mix', 'w_in',
        'ssd_conv_w', 'ssd_conv_b', 'ssd_dt_bias', 'ssd_a_log', 'ssd_d', 'ssd_norm', 'q_norm', 'k_norm',
        'w_br_ssd', 'w_br_att', 'w_out', 'norm_ffn2', 'ffn2_w1', 'ffn2_w3', 'ffn2_w2']


def kernel(**inputs):
    import concourse.bacc as bacc
    from concourse.bass_utils import run_bass_kernel_spmd

    nc = bacc.Bacc("TRN2", target_bir_lowering=False, num_devices=1)
    arrays, args = {}, []
    for name in _INS:
        a = np.ascontiguousarray(inputs[name])
        arrays[f"in_{name}"] = a
        args.append(nc.dram_tensor(f"in_{name}", a.shape, mybir.dt.from_np(a.dtype), kind="ExternalInput").ap())
    out = nc.dram_tensor("out", (1, T, D), F32, kind="ExternalOutput").ap()
    build(nc, *args, out)
    r = run_bass_kernel_spmd(nc, [arrays], core_ids=[0])
    return r.results[0]["out"]
```
